# Optimizing a Trainium2 kernel written in Bass

```python
import math
import jax, jax.numpy as jnp
from jax import lax
import numpy as np

D_MODEL = 1024
BATCH = 1
SEQ = 256
DEPTH = 2

DN_HEADS = 8
DN_DK = 128
DN_DV = 128
DN_CONV = 4
DN_CHUNK = 64
SB_HEADS = 8
SB_DH = 64
SB_BLOCK = 128
D_FF = 3584
N_EXPERTS = 8
TOP_K = 2
MOE_BLOCK = 128
EPS = 1e-6
N_DENSE = (DEPTH + 1) // 2
N_MOE = DEPTH // 2
N_BRANCH = 2

DN_QK = DN_HEADS * DN_DK
DN_V = DN_HEADS * DN_DV
SB_W = SB_HEADS * SB_DH
_WIDTHS = (2 * DN_QK + DN_V, DN_V, DN_HEADS, DN_HEADS, SB_W, SB_W, SB_W, N_BRANCH * D_MODEL)
IN_COLS = sum(_WIDTHS)
SPLIT_AT = tuple(int(s) for s in np.cumsum(_WIDTHS)[:-1])


def rms_norm(x, w):
    xf = x.astype(jnp.float32)
    y = xf * lax.rsqrt(jnp.mean(xf * xf, axis=-1, keepdims=True) + EPS)
    return (y * w.astype(jnp.float32)).astype(x.dtype)

def l2_norm(x):
    xf = x.astype(jnp.float32)
    return xf * lax.rsqrt(jnp.sum(xf * xf, axis=-1, keepdims=True) + EPS)

def causal_depthwise_conv(x, w):
    k = w.shape[0]
    y = lax.conv_general_dilated(x, w[:, None, :].astype(x.dtype), window_strides=(1,),
                                 padding=[(k - 1, 0)], dimension_numbers=('NWC', 'WIO', 'NWC'),
                                 feature_group_count=x.shape[-1])
    return jax.nn.silu(y)

def gated_delta_rule(q, k, v, g, beta):
    B, S, H, DK = q.shape
    DV = v.shape[-1]
    N = S // DN_CHUNK

    def chunk(t):
        return jnp.moveaxis(t.reshape((B, N, DN_CHUNK) + t.shape[2:]), 2, 3)

    q, k, v, g, beta = (chunk(t) for t in (q, k, v, g, beta))
    g = jnp.cumsum(g, axis=-1)
    idx = jnp.arange(DN_CHUNK)
    lower = idx[:, None] >= idx[None, :]
    strict = idx[:, None] > idx[None, :]
    decay = jnp.exp(jnp.where(lower, g[..., :, None] - g[..., None, :], -jnp.inf))
    kk = jnp.einsum('bnhcd,bnhed->bnhce', k, k)
    lmat = jnp.where(strict, beta[..., :, None] * kk * decay, 0.0)
    amat = lmat + jnp.eye(DN_CHUNK, dtype=lmat.dtype)
    rhs = jnp.concatenate([v * beta[..., None], k * (beta * jnp.exp(g))[..., None]], axis=-1)
    sol = lax.linalg.triangular_solve(amat, rhs, left_side=True, lower=True, unit_diagonal=True)
    u, w = sol[..., :DV], sol[..., DV:]
    qk = jnp.einsum('bnhcd,bnhed->bnhce', q, k) * decay
    q_dec = q * jnp.exp(g)[..., None]
    k_dec = k * jnp.exp(g[..., -1:] - g)[..., None]
    g_last = jnp.exp(g[..., -1])

    def step(state, inp):
        qd, kd, u_c, w_c, qk_c, gl = inp
        v_new = u_c - jnp.einsum('bhcd,bhde->bhce', w_c, state)
        o = jnp.einsum('bhcd,bhde->bhce', qd, state) + jnp.einsum('bhcs,bhse->bhce', qk_c, v_new)
        state = state * gl[..., None, None] + jnp.einsum('bhcd,bhce->bhde', kd, v_new)
        return state, o

    xs = tuple(jnp.moveaxis(t, 1, 0) for t in (q_dec, k_dec, u, w, qk, g_last))
    _, o = lax.scan(step, jnp.zeros((B, H, DK, DV), jnp.float32), xs)
    return jnp.transpose(o, (1, 0, 3, 2, 4)).reshape(B, S, H, DV)

def stick_breaking_attention(q, k, v):
    B, S, H, Dh = q.shape
    nq = S // SB_BLOCK
    scale = Dh ** -0.5
    kf = k.astype(jnp.float32)
    vf = v.astype(jnp.float32)
    qb = jnp.moveaxis(q.astype(jnp.float32).reshape(B, nq, SB_BLOCK, H, Dh), 1, 0)
    key_pos = jnp.arange(S)

    def block(args):
        q_blk, i = args
        z = jnp.einsum('bqhd,bkhd->bhqk', q_blk, kf) * scale
        q_pos = i * SB_BLOCK + jnp.arange(SB_BLOCK)
        causal = key_pos[None, :] < q_pos[:, None]
        log_rem = jnp.where(causal, jax.nn.log_sigmoid(-z), 0.0)
        after = lax.cumsum(log_rem, axis=3, reverse=True) - log_rem
        attn = jnp.where(causal, jnp.exp(jax.nn.log_sigmoid(z) + after), 0.0)
        return jnp.einsum('bhqk,bkhd->bqhd', attn, vf)

    o = lax.map(block, (qb, jnp.arange(nq)))
    return jnp.moveaxis(o, 0, 1).reshape(B, S, H, Dh)

def hybrid_mixer(h, w_in, conv_w, a_log, dt_bias, out_norm, w_up_dn, w_up_sb, w_out):
    B, S, _ = h.shape
    proj = h @ w_in
    dn_qkv, dn_z, dn_b, dn_a, sb_q, sb_k, sb_v, gates = jnp.split(proj, SPLIT_AT, axis=-1)
    dn_qkv = causal_depthwise_conv(dn_qkv, conv_w)
    dq, dk, dv = jnp.split(dn_qkv, [DN_QK, 2 * DN_QK], axis=-1)
    q = l2_norm(dq.reshape(B, S, DN_HEADS, DN_DK)) * (DN_DK ** -0.5)
    k = l2_norm(dk.reshape(B, S, DN_HEADS, DN_DK))
    v = dv.reshape(B, S, DN_HEADS, DN_DV).astype(jnp.float32)
    beta = jax.nn.sigmoid(dn_b.astype(jnp.float32))
    g = -jnp.exp(a_log.astype(jnp.float32)) * jax.nn.softplus(dn_a.astype(jnp.float32) + dt_bias.astype(jnp.float32))
    o = gated_delta_rule(q, k, v, g, beta)
    o = rms_norm(o, out_norm) * jax.nn.silu(dn_z.reshape(B, S, DN_HEADS, DN_DV).astype(jnp.float32))
    y_dn = o.reshape(B, S, DN_V).astype(h.dtype) @ w_up_dn
    o_sb = stick_breaking_attention(sb_q.reshape(B, S, SB_HEADS, SB_DH),
                                    sb_k.reshape(B, S, SB_HEADS, SB_DH),
                                    sb_v.reshape(B, S, SB_HEADS, SB_DH))
    y_sb = o_sb.reshape(B, S, SB_W).astype(h.dtype) @ w_up_sb
    g_dn, g_sb = jnp.split(jax.nn.sigmoid(gates), N_BRANCH, axis=-1)
    return (g_dn * y_dn + g_sb * y_sb) @ w_out

def swiglu(h, w1, w3, w2):
    return (jax.nn.silu(h @ w1) * (h @ w3)) @ w2

def moe_swiglu(h, router_w, router_b, w1, w3, w2):
    B, S, D = h.shape
    T = B * S
    hf = h.reshape(T, D)
    logits = (hf @ router_w).astype(jnp.float32) + router_b.astype(jnp.float32)
    top_logit, top_idx = lax.top_k(logits, TOP_K)
    top_w = jax.nn.softmax(top_logit, axis=-1)
    n_assign = T * TOP_K
    flat_e = top_idx.reshape(-1).astype(jnp.int32)
    flat_tok = jnp.arange(n_assign, dtype=jnp.int32) // TOP_K
    order = jnp.argsort(flat_e)
    e_sorted = flat_e[order]
    counts = jnp.bincount(flat_e, length=N_EXPERTS).astype(jnp.int32)
    padded = (counts + MOE_BLOCK - 1) // MOE_BLOCK * MOE_BLOCK
    pad_end = jnp.cumsum(padded)
    pad_start = pad_end - padded
    start = jnp.cumsum(counts) - counts
    dest = pad_start[e_sorted] + jnp.arange(n_assign, dtype=jnp.int32) - start[e_sorted]
    n_rows = (n_assign + N_EXPERTS * (MOE_BLOCK - 1) + MOE_BLOCK - 1) // MOE_BLOCK * MOE_BLOCK
    n_blocks = n_rows // MOE_BLOCK
    row_tok = jnp.full((n_rows,), T, jnp.int32).at[dest].set(flat_tok[order])
    row_w = jnp.zeros((n_rows,), jnp.float32).at[dest].set(top_w.reshape(-1)[order])
    block_start = jnp.arange(n_blocks, dtype=jnp.int32) * MOE_BLOCK
    block_e = jnp.minimum(jnp.sum(pad_end[None, :] <= block_start[:, None], axis=1), N_EXPERTS - 1)
    h_pad = jnp.concatenate([hf, jnp.zeros((1, D), hf.dtype)], axis=0)

    def expert_block(args):
        toks, e = args
        xb = h_pad[toks]
        return (jax.nn.silu(xb @ w1[e]) * (xb @ w3[e])) @ w2[e]

    y = lax.map(expert_block, (row_tok.reshape(n_blocks, MOE_BLOCK), block_e))
    y = y.reshape(n_rows, D) * row_w[:, None].astype(h.dtype)
    out = jax.ops.segment_sum(y, row_tok, num_segments=T + 1)[:T]
    return out.reshape(B, S, D)

def first_inputs(seed: int = 0) -> dict:
    key = jax.random.key(seed)
    ks = jax.random.split(key, 26)
    f32 = jnp.float32

    def nrm(k, shape, scale):
        return jax.random.normal(k, shape, f32) * scale

    L = DEPTH
    dt = jnp.exp(jax.random.uniform(ks[9], (L, DN_HEADS), f32, math.log(1e-3), math.log(1e-1)))
    return {
        "x": nrm(ks[0], (BATCH, SEQ, D_MODEL), 1.0),
        "c": nrm(ks[1], (BATCH, D_MODEL), 1.0),
        "ada_w": nrm(ks[2], (L, D_MODEL, 6 * D_MODEL), 0.5 * D_MODEL ** -0.5),
        "ada_b": nrm(ks[3], (L, 6 * D_MODEL), 0.02),
        "norm_mix": 1.0 + nrm(ks[4], (L, D_MODEL), 0.05),
        "norm_ffn": 1.0 + nrm(ks[5], (L, D_MODEL), 0.05),
        "w_in": nrm(ks[6], (L, D_MODEL, IN_COLS), D_MODEL ** -0.5),
        "conv_w": nrm(ks[7], (L, DN_CONV, 2 * DN_QK + DN_V), DN_CONV ** -0.5),
        "dn_a_log": jnp.log(jax.random.uniform(ks[8], (L, DN_HEADS), f32, 1.0, 16.0)),
        "dn_dt_bias": dt + jnp.log(-jnp.expm1(-dt)),
        "dn_out_norm": 1.0 + nrm(ks[10], (L, DN_DV), 0.05),
        "w_up_dn": nrm(ks[11], (L, DN_V, D_MODEL), DN_V ** -0.5),
        "w_up_sb": nrm(ks[12], (L, SB_W, D_MODEL), SB_W ** -0.5),
        "w_out": nrm(ks[13], (L, D_MODEL, D_MODEL), D_MODEL ** -0.5),
        "ffn_w1": nrm(ks[14], (N_DENSE, D_MODEL, D_FF), D_MODEL ** -0.5),
        "ffn_w3": nrm(ks[15], (N_DENSE, D_MODEL, D_FF), D_MODEL ** -0.5),
        "ffn_w2": nrm(ks[16], (N_DENSE, D_FF, D_MODEL), D_FF ** -0.5),
        "router_w": nrm(ks[17], (N_MOE, D_MODEL, N_EXPERTS), D_MODEL ** -0.5),
        "router_b": nrm(ks[18], (N_MOE, N_EXPERTS), 0.01),
        "moe_w1": nrm(ks[19], (N_MOE, N_EXPERTS, D_MODEL, D_FF), D_MODEL ** -0.5),
        "moe_w3": nrm(ks[20], (N_MOE, N_EXPERTS, D_MODEL, D_FF), D_MODEL ** -0.5),
        "moe_w2": nrm(ks[21], (N_MOE, N_EXPERTS, D_FF, D_MODEL), D_FF ** -0.5),
        "final_norm": 1.0 + nrm(ks[22], (D_MODEL,), 0.05),
    }

def first_block(x, c, ada_w, ada_b, norm_mix, norm_ffn, w_in, conv_w, dn_a_log, dn_dt_bias,
              dn_out_norm, w_up_dn, w_up_sb, w_out, ffn_w1, ffn_w3, ffn_w2, router_w, router_b,
              moe_w1, moe_w3, moe_w2, final_norm):
    c_act = jax.nn.silu(c)
    for l in range(DEPTH):
        mod = (c_act @ ada_w[l] + ada_b[l])[:, None, :]
        sh1, sc1, gt1, sh2, sc2, gt2 = jnp.split(mod, 6, axis=-1)
        h = rms_norm(x, norm_mix[l]) * (1.0 + sc1) + sh1
        x = x + gt1 * hybrid_mixer(h, w_in[l], conv_w[l], dn_a_log[l], dn_dt_bias[l], dn_out_norm[l],
                                   w_up_dn[l], w_up_sb[l], w_out[l])
        h = rms_norm(x, norm_ffn[l]) * (1.0 + sc2) + sh2
        if l % 2 == 0:
            f = swiglu(h, ffn_w1[l // 2], ffn_w3[l // 2], ffn_w2[l // 2])
        else:
            j = l // 2
            f = moe_swiglu(h, router_w[j], router_b[j], moe_w1[j], moe_w3[j], moe_w2[j])
        x = x + gt2 * f
    return rms_norm(x, final_norm)


DEPTH_2 = 1

N_MEM = 256

SSD_D_INNER = D_MODEL
SSD_HEAD_DIM = 64
SSD_HEADS = SSD_D_INNER // SSD_HEAD_DIM
SSD_GROUPS = 4
SSD_HEADS_PER_GROUP = SSD_HEADS // SSD_GROUPS
SSD_STATE = 128
SSD_CONV = 4
SSD_CHUNK = 128
SSD_CONV_DIM = SSD_D_INNER + 2 * SSD_GROUPS * SSD_STATE

DIL_PAIRS = ((128, 1), (512, 4), (2048, 16))
DIL_HEADS_PER_GROUP = 4
DIL_HEAD_DIM = 64
DIL_HEADS = len(DIL_PAIRS) * DIL_HEADS_PER_GROUP
DIL_WIDTH = DIL_HEADS * DIL_HEAD_DIM
DIL_OUT_WIDTH = DIL_HEADS_PER_GROUP * DIL_HEAD_DIM

MEM_HEADS = 4
MEM_HEAD_DIM = 192
MEM_WIDTH = MEM_HEADS * MEM_HEAD_DIM

ROPE_THETA = 500000.0
ROPE_FRACTION = 4

PEER_HEADS = 8
PEER_N_KEYS = 128
PEER_EXPERTS = PEER_N_KEYS * PEER_N_KEYS
PEER_QUERY_DIM = 256
PEER_TOPK = 16
PEER_BLOCK = 64

N_BRANCHES = 3

OFF_Z = 0
OFF_XBC = OFF_Z + SSD_D_INNER
OFF_DT = OFF_XBC + SSD_CONV_DIM
OFF_DQ = OFF_DT + SSD_HEADS
OFF_DK = OFF_DQ + DIL_WIDTH
OFF_DV = OFF_DK + DIL_WIDTH
OFF_MQ = OFF_DV + DIL_WIDTH
OFF_GATE = OFF_MQ + MEM_WIDTH
IN_PROJ_WIDTH = OFF_GATE + N_BRANCHES * D_MODEL


F32 = jnp.float32

def _rms_norm(t, w):
    tf = t.astype(F32)
    tf = tf * lax.rsqrt(jnp.mean(tf * tf, axis=-1, keepdims=True) + EPS)
    return (tf * w.astype(F32)).astype(t.dtype)

def _partial_rope(t, positions):
    hd = t.shape[-1]
    rot = hd // ROPE_FRACTION
    half = rot // 2
    inv = jnp.exp(-math.log(ROPE_THETA) * (2.0 / rot) * jnp.arange(half, dtype=F32))
    ang = positions.astype(F32)[..., None] * inv
    cos = jnp.cos(ang)[:, :, None, :]
    sin = jnp.sin(ang)[:, :, None, :]
    tf = t.astype(F32)
    t1 = tf[..., :half]
    t2 = tf[..., half:rot]
    out = jnp.concatenate([t1 * cos - t2 * sin, t2 * cos + t1 * sin, tf[..., rot:]], axis=-1)
    return out.astype(t.dtype)

def _causal_depthwise_conv(t, w, bias):
    c = t.shape[-1]
    y = lax.conv_general_dilated(
        t, w[:, None, :].astype(t.dtype), window_strides=(1,),
        padding=[(w.shape[0] - 1, 0)],
        dimension_numbers=('NWC', 'WIO', 'NWC'),
        feature_group_count=c)
    return y + bias.astype(t.dtype)

def _ssd_chunked(xh, dt, a, bmat, cmat):
    b, s, g, r, p = xh.shape
    n = bmat.shape[-1]
    nc = s // SSD_CHUNK
    x_dt = xh.astype(F32) * dt[..., None]
    da = dt * a

    def chunks(t):
        return jnp.moveaxis(t.reshape(b, nc, SSD_CHUNK, *t.shape[2:]), 1, 0)

    tril = jnp.tril(jnp.ones((SSD_CHUNK, SSD_CHUNK), dtype=bool))
    strict = jnp.tril(jnp.ones((SSD_CHUNK, SSD_CHUNK), dtype=bool), k=-1)

    def step(state, inp):
        xc, dac, bc, cc = inp
        dat = jnp.moveaxis(dac, 1, -1)
        acum = jnp.cumsum(dat, axis=-1)
        seg = jnp.cumsum(jnp.where(strict, dat[..., :, None], 0.0), axis=-2)
        lmat = jnp.exp(jnp.where(tril, seg, -jnp.inf))
        cb = jnp.einsum('bsgn,btgn->bgst', cc, bc)
        y_diag = jnp.einsum('bgst,bgrst,btgrp->bsgrp', cb, lmat, xc)
        y_off = jnp.einsum('bsgn,bgrpn,bgrs->bsgrp', cc, state, jnp.exp(acum))
        decay = jnp.exp(acum[..., -1:] - acum)
        new_state = (state * jnp.exp(acum[..., -1])[..., None, None]
                     + jnp.einsum('btgn,bgrt,btgrp->bgrpn', bc, decay, xc))
        return new_state, y_diag + y_off

    state0 = jnp.zeros((b, g, r, p, n), F32)
    _, ys = lax.scan(step, state0, (chunks(x_dt), chunks(da),
                                    chunks(bmat.astype(F32)), chunks(cmat.astype(F32))))
    return jnp.moveaxis(ys, 0, 1).reshape(b, s, g, r, p)

def _dilated_group_attention(q, k, v, dilation, n_back):
    b, s, h, hd = q.shape
    m = s // dilation
    blk = n_back
    nb = -(-m // blk)
    mp = nb * blk

    def to_sub(t):
        t = t.reshape(b, m, dilation, h, hd)
        t = jnp.pad(t, ((0, 0), (0, mp - m), (0, 0), (0, 0), (0, 0)))
        return t.reshape(b, nb, blk, dilation, h, hd)

    def with_prev(t):
        prev = jnp.pad(t[:, :-1], ((0, 0), (1, 0), (0, 0), (0, 0), (0, 0), (0, 0)))
        return jnp.concatenate([prev, t], axis=2)

    qs = to_sub(q)
    kk = with_prev(to_sub(k))
    vv = with_prev(to_sub(v))
    scores = jnp.einsum('bnqrhd,bnkrhd->bnrhqk', qs, kk).astype(F32) * (hd ** -0.5)
    qi = jnp.arange(blk)[:, None]
    ki = jnp.arange(2 * blk)[None, :]
    dist = qi + blk - ki
    band = (dist >= 0) & (dist <= n_back)
    valid = band[None] & ((jnp.arange(nb)[:, None, None] > 0) | (ki >= blk)[None])
    scores = jnp.where(valid[None, :, None, None], scores, -jnp.inf)
    lse = jax.nn.logsumexp(scores, axis=-1)
    probs = jnp.exp(scores - lse[..., None]).astype(v.dtype)
    out = jnp.einsum('bnrhqk,bnkrhd->bnqrhd', probs, vv)
    out = out.reshape(b, mp, dilation, h, hd)[:, :m].reshape(b, s, h, hd)
    lse = lse.transpose(0, 1, 4, 2, 3).reshape(b, mp, dilation, h)[:, :m].reshape(b, s, h)
    return out, lse

def _peer(hn, w_query, sub_keys, expert_down, expert_up):
    b, s, d = hn.shape
    q = (hn @ w_query).reshape(b, s, PEER_HEADS, 2, PEER_QUERY_DIM // 2)
    sc = jnp.einsum('bshcd,hckd->bshck', q, sub_keys).astype(F32)
    v1, i1 = lax.top_k(sc[..., 0, :], PEER_TOPK)
    v2, i2 = lax.top_k(sc[..., 1, :], PEER_TOPK)
    cand = (v1[..., :, None] + v2[..., None, :]).reshape(b, s, PEER_HEADS, PEER_TOPK * PEER_TOPK)
    cidx = (i1[..., :, None] * PEER_N_KEYS + i2[..., None, :]).reshape(b, s, PEER_HEADS, PEER_TOPK * PEER_TOPK)
    top, pos = lax.top_k(cand, PEER_TOPK)
    idx = jnp.take_along_axis(cidx, pos, axis=-1)
    gate = jax.nn.softmax(top, axis=-1)
    nblk = s // PEER_BLOCK

    def blockify(t):
        return jnp.moveaxis(t.reshape(b, nblk, PEER_BLOCK, *t.shape[2:]), 1, 0)

    def one_block(args):
        hb, ib, gb = args
        u = expert_down[ib]
        act = jax.nn.gelu(jnp.einsum('bld,blhkd->blhk', hb, u), approximate=False)
        coef = (gb * act.astype(F32)).astype(hb.dtype)
        vv = expert_up[ib]
        return jnp.einsum('blhk,blhkd->bld', coef, vv)

    out = lax.map(one_block, (blockify(hn), blockify(idx), blockify(gate)))
    return jnp.moveaxis(out, 0, 1).reshape(b, s, d)

def second_inputs(seed: int = 0) -> dict:
    key = jax.random.key(seed)
    ks = jax.random.split(key, 32)
    L = DEPTH_2

    def nrm(k, shape, scale):
        return jax.random.normal(k, shape, F32) * scale

    def gain(k, shape):
        return 1.0 + 0.05 * jax.random.normal(k, shape, F32)

    x = nrm(ks[0], (BATCH, SEQ, D_MODEL), 1.0)
    mem = nrm(ks[1], (BATCH, N_MEM, D_MODEL), 1.0)
    offset = jax.random.randint(ks[2], (BATCH, 1), 0, 4096, dtype=jnp.int32)
    positions = jnp.arange(SEQ, dtype=jnp.int32)[None, :] + offset
    norm_mix_w = gain(ks[3], (L, D_MODEL))
    w_in = nrm(ks[4], (L, D_MODEL, IN_PROJ_WIDTH), D_MODEL ** -0.5)
    ssd_conv_w = nrm(ks[5], (L, SSD_CONV, SSD_CONV_DIM), SSD_CONV ** -0.5)
    ssd_conv_b = nrm(ks[6], (L, SSD_CONV_DIM), 0.02)
    dt0 = jnp.exp(jax.random.uniform(ks[7], (L, SSD_HEADS), F32, math.log(1e-3), math.log(1e-1)))
    ssd_dt_bias = dt0 + jnp.log(-jnp.expm1(-dt0))
    ssd_a_log = jnp.log(jax.random.uniform(ks[8], (L, SSD_HEADS), F32, 1.0, 16.0))
    ssd_d = gain(ks[9], (L, SSD_HEADS))
    ssd_norm_w = gain(ks[10], (L, SSD_D_INNER))
    dil_q_norm_w = gain(ks[11], (L, DIL_HEAD_DIM))
    dil_k_norm_w = gain(ks[12], (L, DIL_HEAD_DIM))
    mem_norm_w = gain(ks[13], (L, D_MODEL))
    w_mem_kv = nrm(ks[14], (L, D_MODEL, 2 * MEM_WIDTH), D_MODEL ** -0.5)
    mem_q_norm_w = gain(ks[15], (L, MEM_HEAD_DIM))
    mem_k_norm_w = gain(ks[16], (L, MEM_HEAD_DIM))
    w_ssd_br = nrm(ks[17], (L, SSD_D_INNER, D_MODEL), SSD_D_INNER ** -0.5)
    w_dil_br = nrm(ks[18], (L, DIL_OUT_WIDTH, D_MODEL), DIL_OUT_WIDTH ** -0.5)
    w_mem_br = nrm(ks[19], (L, MEM_WIDTH, D_MODEL), MEM_WIDTH ** -0.5)
    w_out = nrm(ks[20], (L, D_MODEL, D_MODEL), D_MODEL ** -0.5)
    norm_ffn_w = gain(ks[21], (L, D_MODEL))
    peer_w_query = nrm(ks[22], (L, D_MODEL, PEER_HEADS * PEER_QUERY_DIM), D_MODEL ** -0.5)
    peer_sub_keys = nrm(ks[23], (L, PEER_HEADS, 2, PEER_N_KEYS, PEER_QUERY_DIM // 2),
                        (PEER_QUERY_DIM // 2) ** -0.5)
    peer_down = nrm(ks[24], (L, PEER_EXPERTS, D_MODEL), D_MODEL ** -0.5)
    peer_up = nrm(ks[25], (L, PEER_EXPERTS, D_MODEL), PEER_HEADS ** -0.5)
    return {
        'x': x, 'mem': mem, 'positions': positions,
        'norm_mix_w': norm_mix_w, 'w_in': w_in,
        'ssd_conv_w': ssd_conv_w, 'ssd_conv_b': ssd_conv_b, 'ssd_dt_bias': ssd_dt_bias,
        'ssd_a_log': ssd_a_log, 'ssd_d': ssd_d, 'ssd_norm_w': ssd_norm_w,
        'dil_q_norm_w': dil_q_norm_w, 'dil_k_norm_w': dil_k_norm_w,
        'mem_norm_w': mem_norm_w, 'w_mem_kv': w_mem_kv,
        'mem_q_norm_w': mem_q_norm_w, 'mem_k_norm_w': mem_k_norm_w,
        'w_ssd_br': w_ssd_br, 'w_dil_br': w_dil_br, 'w_mem_br': w_mem_br, 'w_out': w_out,
        'norm_ffn_w': norm_ffn_w, 'peer_w_query': peer_w_query, 'peer_sub_keys': peer_sub_keys,
        'peer_down': peer_down, 'peer_up': peer_up,
    }

def second_block(x, mem, positions, norm_mix_w, w_in, ssd_conv_w, ssd_conv_b, ssd_dt_bias,
              ssd_a_log, ssd_d, ssd_norm_w, dil_q_norm_w, dil_k_norm_w, mem_norm_w, w_mem_kv,
              mem_q_norm_w, mem_k_norm_w, w_ssd_br, w_dil_br, w_mem_br, w_out, norm_ffn_w,
              peer_w_query, peer_sub_keys, peer_down, peer_up):
    b, s, _ = x.shape
    n_mem = mem.shape[1]
    h = x
    for layer in range(DEPTH_2):
        u = _rms_norm(h, norm_mix_w[layer])
        proj = u @ w_in[layer]
        z = proj[..., OFF_Z:OFF_XBC]
        xbc = proj[..., OFF_XBC:OFF_DT]
        dt_raw = proj[..., OFF_DT:OFF_DQ]
        dq = proj[..., OFF_DQ:OFF_DK].reshape(b, s, DIL_HEADS, DIL_HEAD_DIM)
        dk = proj[..., OFF_DK:OFF_DV].reshape(b, s, DIL_HEADS, DIL_HEAD_DIM)
        dv = proj[..., OFF_DV:OFF_MQ].reshape(b, s, DIL_HEADS, DIL_HEAD_DIM)
        mq = proj[..., OFF_MQ:OFF_GATE].reshape(b, s, MEM_HEADS, MEM_HEAD_DIM)
        gates = jax.nn.sigmoid(proj[..., OFF_GATE:].astype(F32)).reshape(b, s, N_BRANCHES, D_MODEL)

        xbc = jax.nn.silu(_causal_depthwise_conv(xbc, ssd_conv_w[layer], ssd_conv_b[layer]))
        gn = SSD_GROUPS * SSD_STATE
        xs = xbc[..., :SSD_D_INNER].reshape(b, s, SSD_GROUPS, SSD_HEADS_PER_GROUP, SSD_HEAD_DIM)
        bm = xbc[..., SSD_D_INNER:SSD_D_INNER + gn].reshape(b, s, SSD_GROUPS, SSD_STATE)
        cm = xbc[..., SSD_D_INNER + gn:].reshape(b, s, SSD_GROUPS, SSD_STATE)
        dt = jax.nn.softplus(dt_raw.astype(F32) + ssd_dt_bias[layer].astype(F32))
        dt = dt.reshape(b, s, SSD_GROUPS, SSD_HEADS_PER_GROUP)
        a = -jnp.exp(ssd_a_log[layer].astype(F32)).reshape(SSD_GROUPS, SSD_HEADS_PER_GROUP)
        y = _ssd_chunked(xs, dt, a, bm, cm)
        y = y + ssd_d[layer].astype(F32).reshape(SSD_GROUPS, SSD_HEADS_PER_GROUP)[..., None] * xs.astype(F32)
        y = y.reshape(b, s, SSD_D_INNER) * jax.nn.silu(z.astype(F32))
        yg = y.reshape(b, s, SSD_GROUPS, SSD_D_INNER // SSD_GROUPS)
        yg = yg * lax.rsqrt(jnp.mean(yg * yg, axis=-1, keepdims=True) + EPS)
        y_ssd = (yg.reshape(b, s, SSD_D_INNER) * ssd_norm_w[layer].astype(F32)).astype(h.dtype)

        dq = _partial_rope(_rms_norm(dq, dil_q_norm_w[layer]), positions)
        dk = _partial_rope(_rms_norm(dk, dil_k_norm_w[layer]), positions)
        outs = []
        lses = []
        for gi, (window, dilation) in enumerate(DIL_PAIRS):
            sl = slice(gi * DIL_HEADS_PER_GROUP, (gi + 1) * DIL_HEADS_PER_GROUP)
            o, l = _dilated_group_attention(dq[:, :, sl], dk[:, :, sl], dv[:, :, sl],
                                            dilation, window // dilation)
            outs.append(o.astype(F32))
            lses.append(l)
        wts = jax.nn.softmax(jnp.stack(lses, axis=0), axis=0)
        y_dil = jnp.sum(wts[..., None] * jnp.stack(outs, axis=0), axis=0)
        y_dil = y_dil.reshape(b, s, DIL_OUT_WIDTH).astype(h.dtype)

        mkv = _rms_norm(mem, mem_norm_w[layer]) @ w_mem_kv[layer]
        mk = mkv[..., :MEM_WIDTH].reshape(b, n_mem, MEM_HEADS, MEM_HEAD_DIM)
        mv = mkv[..., MEM_WIDTH:].reshape(b, n_mem, MEM_HEADS, MEM_HEAD_DIM)
        mqn = _rms_norm(mq, mem_q_norm_w[layer])
        mk = _rms_norm(mk, mem_k_norm_w[layer])
        msc = jnp.einsum('bshd,bmhd->bhsm', mqn, mk).astype(F32) * (MEM_HEAD_DIM ** -0.5)
        mp = jax.nn.softmax(msc, axis=-1).astype(mv.dtype)
        y_mem = jnp.einsum('bhsm,bmhd->bshd', mp, mv).reshape(b, s, MEM_WIDTH)

        merged = (gates[:, :, 0] * (y_ssd @ w_ssd_br[layer]).astype(F32)
                  + gates[:, :, 1] * (y_dil @ w_dil_br[layer]).astype(F32)
                  + gates[:, :, 2] * (y_mem @ w_mem_br[layer]).astype(F32))
        h = h + merged.astype(h.dtype) @ w_out[layer]

        hn = _rms_norm(h, norm_ffn_w[layer])
        h = h + _peer(hn, peer_w_query[layer], peer_sub_keys[layer], peer_down[layer], peer_up[layer])
    return h


def setup_inputs(seed=0):
    out = dict(first_inputs(seed))
    for name, value in second_inputs(seed + 1).items():
        if name != "x":
            out[name + "_2"] = value
    return out


def reference(
    x, c, ada_w, ada_b, norm_mix, norm_ffn, w_in, conv_w, dn_a_log, dn_dt_bias, dn_out_norm,
    w_up_dn, w_up_sb, w_out, ffn_w1, ffn_w3, ffn_w2, router_w, router_b, moe_w1, moe_w3, moe_w2,
    final_norm, mem_2, positions_2, norm_mix_w_2, w_in_2, ssd_conv_w_2, ssd_conv_b_2,
    ssd_dt_bias_2, ssd_a_log_2, ssd_d_2, ssd_norm_w_2, dil_q_norm_w_2, dil_k_norm_w_2,
    mem_norm_w_2, w_mem_kv_2, mem_q_norm_w_2, mem_k_norm_w_2, w_ssd_br_2, w_dil_br_2,
    w_mem_br_2, w_out_2, norm_ffn_w_2, peer_w_query_2, peer_sub_keys_2, peer_down_2, peer_up_2,
):
    x = first_block(
        x, c, ada_w, ada_b, norm_mix, norm_ffn, w_in, conv_w, dn_a_log, dn_dt_bias, dn_out_norm,
        w_up_dn, w_up_sb, w_out, ffn_w1, ffn_w3, ffn_w2, router_w, router_b, moe_w1, moe_w3,
        moe_w2, final_norm,
    )
    return second_block(
        x, mem_2, positions_2, norm_mix_w_2, w_in_2, ssd_conv_w_2, ssd_conv_b_2, ssd_dt_bias_2,
        ssd_a_log_2, ssd_d_2, ssd_norm_w_2, dil_q_norm_w_2, dil_k_norm_w_2, mem_norm_w_2,
        w_mem_kv_2, mem_q_norm_w_2, mem_k_norm_w_2, w_ssd_br_2, w_dil_br_2, w_mem_br_2, w_out_2,
        norm_ffn_w_2, peer_w_query_2, peer_sub_keys_2, peer_down_2, peer_up_2,
    )


_drawn_inputs = setup_inputs


def setup_inputs(seed=0):
    import zlib

    import numpy as np

    out = dict(_drawn_inputs(seed))
    spreads = {}
    factors = {'dn_out_norm': 2.702,
     'router_b': 3.534,
     'dil_q_norm_w_2': 5.625,
     'dil_k_norm_w_2': 4.982,
     'mem_norm_w_2': 5.187,
     'mem_q_norm_w_2': 7.384,
     'mem_k_norm_w_2': 6.007,
     'ssd_conv_b_2': 8.0,
     'ssd_d_2': 8.0,
     'ssd_norm_w_2': 5.355,
     'norm_ffn_w_2': 3.814}
    for name, (base, spread) in spreads.items():
        noise = np.random.default_rng([zlib.crc32(name.encode()), seed]).standard_normal(out[name].shape)
        drawn = base * np.exp(spread * noise) if base else spread * noise
        out[name] = __import__('jax').numpy.asarray(drawn.astype(out[name].dtype))
    for name, factor in factors.items():
        out[name] = (out[name] * factor).astype(out[name].dtype)
    return out
```

```python
from contextlib import ExitStack

import numpy as np
import concourse.bass as bass
from concourse import mybir

F32 = mybir.dt.float32
U32 = mybir.dt.uint32
I32 = mybir.dt.int32
ALU = mybir.AluOpType
ACT = mybir.ActivationFunctionType
AX = mybir.AxisListType

P = 128
T = 256
TT = T // P
D = 1024
KC = D // P
EPS = 1e-6
NEG = -1.0e30
R = 3
SLOT = 4096
NSIG = 24

L = 2
DNH = 8
SBH = 8
FF = 3584
NE = 8
IN_COLS = 7696
BA = 4096
IN_B = BA + 16
Q0, K0, V0, Z0, SQ0, SK0, SV0, GD0, GS0 = 0, 8, 16, 24, 32, 36, 40, 44, 52
NBLK1 = 60

N_MEM = 256
SSH = 16
SSG = 4
IN2_COLS = 9232
DT0 = 3072
IN2_B = DT0 + 16
ZZ0, XS0, BM0, CM0, DQ0, DK0, DV0, MQ0, G20 = 0, 8, 16, 20, 24, 30, 36, 42, 48
NBLK2 = 72
DILH = 12
MH = 4
MD = 192
ROPE_THETA = 500000.0
PH = 8
NK = 128
TOPK = 16


def constants():
    a = np.arange(P)
    s, t = a[:, None], a[None, :]
    neg = np.float32(NEG)
    cols = {
        "ident": s == t,
        "ones": np.ones((P, P)),
        "tri_ge": s >= t,
        "neg_le": np.where(s <= t, 0, neg),
        "msk_lt": s < t,
        "neg_lt": np.where(s < t, 0, neg),
        "ones64": s // 64 == t // 64,
        "iota": np.broadcast_to(t, (P, P)),
    }
    perm = np.zeros((P, P))
    for p in range(P):
        d = p % 64
        if d < 8:
            perm[p + 8, p] = -1
        elif d < 16:
            perm[p - 8, p] = 1
    cols["perm"] = perm
    inv = np.exp(np.float32(-np.log(ROPE_THETA) * (2.0 / 16)) * np.arange(8, dtype=np.float32)).astype(np.float32)
    invc = np.zeros((P, 1))
    for p in range(P):
        if p % 64 < 16:
            invc[p, 0] = inv[p % 64 % 8]
    cols["inv"] = invc
    main = np.concatenate([np.asarray(v, np.float32) for v in cols.values()], axis=1)
    at, off = {}, 0
    for n, v in cols.items():
        w = np.asarray(v).shape[1]
        at[n] = (off, w)
        off += w
    level = []
    w = 1
    while w < P:
        level.append((s // (2 * w) == t // (2 * w)) & (s % (2 * w) < w) & (t % (2 * w) >= w))
        w *= 2
    level = np.concatenate([np.asarray(v, np.float32) for v in level], axis=1)
    head = np.arange(3 * P) // MD
    memh = np.concatenate([(head[b * P:(b + 1) * P, None] == head[None, c * P:(c + 1) * P]).astype(np.float32)
                           for b in range(3) for c in range(3)], axis=1)
    dil = []
    for tile, width in ((0, P), (1, T)):
        tq = tile * P + a[:, None]
        sk = np.arange(width)[None, :]
        for step, back in ((1, 128), (4, 512), (16, 2048)):
            dist = tq - sk
            dil.append(np.where((dist >= 0) & (dist % step == 0) & (dist <= back), 0, neg))
    dil = np.concatenate([np.asarray(v, np.float32) for v in dil], axis=1)
    return main, at, level, memh, dil


class Chain:

    def __init__(self, eng, sem):
        self.eng, self.sem, self.n = eng, sem, 0

    def __call__(self, ins):
        ins.then_inc(self.sem, 1)
        self.n += 1
        self.eng.wait_ge(self.sem, self.n)


class Kern:

    def __init__(self, nc, ctx, a):
        self.nc, self.ctx, self.a = nc, ctx, a
        self.banks = [[ctx.enter_context(nc.semaphore(f"stage{p}_signal{i}")) for i in range(NSIG)] for p in range(2)]
        self.stage_no = 0
        self.loaded = [ctx.enter_context(nc.semaphore(f"weights_loaded{s}")) for s in range(R)]
        self.used = ctx.enter_context(nc.semaphore("weights_used"))
        self.params_in = ctx.enter_context(nc.semaphore("params_in"))
        self.groups, self.start, self.value = [], {}, []
        self.slot_count = [0] * R
        self.ps = ctx.enter_context(nc.psum_tensor("psum_all", [P, 8, 512], F32))
        self.issued = 0

    def sb(self, name, shape, dt=F32, ctx=None):
        return (ctx or self.ctx).enter_context(self.nc.sbuf_tensor(name, shape, dt))

    def add_group(self, name, n, loads, each=1):
        g0 = len(self.value)
        self.start[name] = g0
        self.groups.append((name, g0, n, loads, each))
        for g in range(g0, g0 + n):
            self.slot_count[g % R] += 16 * each
            self.value.append(self.slot_count[g % R])

    def load_value(self, g, it=0, each=1):
        return self.value[g] + it * (16 * each)

    def issue(self, sp, upto):
        upto = min(upto, len(self.value))
        for name, g0, n, loads, each in self.groups:
            lo, hi = max(self.issued, g0), min(upto, g0 + n)
            if lo >= hi:
                continue

            def one(q, it, g0=g0, loads=loads):
                g = g0 + q
                wait = it * R + (g - R + 1)
                if not isinstance(wait, int) or wait > 0:
                    sp.wait_ge(self.used, wait)
                for dst, src in loads(q, it, self.ring[:, g % R]):
                    sp.dma_start(dst, src).then_inc(self.loaded[g % R], 16)

            i = lo - g0
            end = hi - g0
            while i < end and i % R:
                one(i % R, i // R)
                i += 1
            full = (end - i) // R
            if full >= 2:
                with sp.Fori(i // R, i // R + full) as it:
                    for q in range(R):
                        one(q, it)
                i += full * R
            while i < end:
                one(i % R, i // R)
                i += 1
        self.issued = max(self.issued, upto)

    def stage(self, name):
        return Stage(self, name)


class Stage:
    def __init__(self, k, name):
        self.k, self.name = k, name

    def __enter__(self):
        k = self.k
        self.ctx = ExitStack()
        self.sems = iter(k.banks[k.stage_no % 2])
        self.block = self.ctx.enter_context(k.nc.Block())
        other = k.banks[(k.stage_no + 1) % 2]
        self.cleared = other
        k.stage_no += 1
        return self

    def signals(self, n):
        return [next(self.sems) for _ in range(n)]

    def clear_last(self, pool):
        for s in self.cleared:
            pool.sem_clear(s)

    def __exit__(self, *e):
        return self.ctx.__exit__(*e)


def over_rounds(eng, n, body):
    full = n // R
    if full >= 2:
        with eng.Fori(0, full) as it:
            for q in range(R):
                body(q, it)
    else:
        for it in range(full):
            for q in range(R):
                body(q, it)
    for i in range(full * R, n):
        body(i % R, i // R)


def half(ps, b):
    return ps[:, b // 2, (b % 2) * T:(b % 2) * T + T]


def linear(k, group, n, h, dest, blk0, each=1, ahead=R):
    g0 = k.start[group]
    with k.stage(group) as st:
        block = st.block
        psum_free, copied = st.signals(2)

        @block.gpsimd
        def _(pool):
            st.clear_last(pool)

        @block.sync
        def _(sp):
            k.issue(sp, g0 + n + ahead)

        @block.tensor
        def _(pe):
            def panel(q, it):
                s = (g0 + q) % R
                pe.wait_ge(k.loaded[s], k.load_value(g0 + q, it, each))
                pe.wait_ge(psum_free, it * R + (q + 1))
                w = k.ring[:, s].rearrange("p (c n) -> p c n", c=KC)
                for j in range(4):
                    for c in range(KC):
                        mm = pe.matmul(half(k.ps, 4 * s + j), w[:, c, j * P:(j + 1) * P], h[:, c],
                                       start=(c == 0), stop=(c == KC - 1))
                mm.then_inc(k.used, 1)
            over_rounds(pe, n, panel)

        @block.scalar
        def _(act):
            act.sem_inc(psum_free, R)

            def panel(q, it):
                s = (g0 + q) % R
                act.wait_ge(k.used, it * R + (g0 + q + 1))
                src = k.ps[:, 2 * s:2 * s + 2, :].rearrange("p b (j t) -> p (b j) t", j=2)
                act.activation(dest[:, bass.ds(it * (4 * R) + (blk0 + 4 * q), 4)], src, ACT.Copy).then_inc(psum_free, 1)
            over_rounds(act, n, panel)


def row_bc(ap, n):
    return ap.unsqueeze(1).to_broadcast([ap.shape[0], n, ap.shape[1]])


def col_bc(ap, n):
    return ap.unsqueeze(2).to_broadcast([ap.shape[0], ap.shape[1], n])


def place_rows(ps, rows, p0=0):
    return ps[p0:p0 + rows, :, :].rearrange("p b (j t) -> p (b j) t", j=2)


PARAMS = [
    (0, 0, 48, "ada_b0", "ada_b", 0), (0, 48, 8, "norm_mix0", "norm_mix", 0), (0, 56, 8, "norm_ffn0", "norm_ffn", 0),
    (0, 64, 1, "out_norm0", "dn_out_norm", 0), (0, 65, 8, "c", "c", 0), (0, 73, 8, "final_norm", "final_norm", None),
    (1, 0, 48, "ada_b1", "ada_b", 1), (1, 48, 8, "norm_mix1", "norm_mix", 1), (1, 56, 8, "norm_ffn1", "norm_ffn", 1),
    (1, 64, 1, "out_norm1", "dn_out_norm", 1), (1, 65, 8, "norm_mix_2", "norm_mix_w_2", 0),
    (1, 73, 8, "ssd_norm_2", "ssd_norm_w_2", 0), (1, 81, 8, "mem_norm_2", "mem_norm_w_2", 0),
    (1, 89, 8, "norm_ffn_2", "norm_ffn_w_2", 0),
    (2, 0, 96, "conv0", "conv_w", 0), (3, 0, 96, "conv1", "conv_w", 1),
    (4, 0, 64, "conv_2", "ssd_conv_w_2", 0), (4, 64, 16, "conv_b_2", "ssd_conv_b_2", 0),
]
NPT = 5


def prologue(k):
    a = k.a
    with ExitStack() as ctx:
        rows = k.sb("param_rows", [P, NPT, P], ctx=ctx)
        xrow = k.sb("x_rows", [P, TT, D], ctx=ctx)
        skip = k.sb("ssd_skip", [P, SSH], ctx=ctx)
        with k.stage("prologue") as st:
            block = st.block
            in_tables, in_rows, in_x, rows_zero, turned, moved, exp_a = st.signals(7)
            n_rows = [0]

            @block.gpsimd
            def _(pool):
                pool.memset(rows[:], 0.0).then_inc(rows_zero, 1)

            @block.sync
            def _(sp):
                sp.dma_start(k.tables[:], a["table_main"]).then_inc(in_tables, 16)
                sp.dma_start(xrow[:], a["x"][0].rearrange("(i p) d -> p i d", p=P)).then_inc(in_x, 16)
                k.issue(sp, R)
                sp.wait_ge(rows_zero, 1)

                def load(dst, src):
                    sp.dma_start(dst, src).then_inc(in_rows, 16)
                    n_rows[0] += 16
                for tile, r0, n, name, src, layer in PARAMS:
                    v = a[src] if layer is None else a[src][layer]
                    v = v.rearrange("j (b p) -> (j b) p", p=P) if len(v.shape) == 2 else v.rearrange("(b p) -> b p", p=P)
                    load(rows[r0:r0 + n, tile, :], v)
                    k.col_at[name] = (tile, r0)
                for r, src in ((80, "dil_q_norm_w_2"), (81, "dil_k_norm_w_2")):
                    for e in range(2):
                        load(rows[r:r + 1, 4, 64 * e:64 * e + 64], a[src])
                for r, src in ((82, "mem_q_norm_w_2"), (85, "mem_k_norm_w_2")):
                    for i, (c0, w0, n) in enumerate(((0, 0, 128), (0, 128, 64), (64, 0, 64), (0, 64, 128))):
                        row = r + (0, 1, 1, 2)[i]
                        load(rows[row:row + 1, 4, c0:c0 + n], a[src][:, w0:w0 + n])
                load(skip[:], a["ssd_d_2"].to_broadcast([P, SSH]))
                k.col_at.update(dil_q=(4, 80), dil_k=(4, 81), mem_q=(4, 82), mem_k=(4, 85), ssd_d=(4, 88))
                for l in range(L):
                    load(k.hp[0:DNH, 2 * l:2 * l + 1], a["dn_a_log"][l].unsqueeze(1))
                    load(k.hp[0:DNH, 2 * l + 1:2 * l + 2], a["dn_dt_bias"][l].unsqueeze(1))
                    load(k.wba[:, l], a["w_in"][l].rearrange("(c p) n -> p c n", p=P)[:, :, BA:BA + 16])
                load(k.hp[0:SSH, 4:5], a["ssd_a_log_2"][0].unsqueeze(1))
                load(k.hp[0:SSH, 5:6], a["ssd_dt_bias_2"][0].unsqueeze(1))
                load(k.wdt[:], a["w_in_2"][0].rearrange("(c p) n -> p c n", p=P)[:, :, DT0:DT0 + 16])
                load(k.wrt[:], a["router_w"][0].rearrange("(c p) n -> p c n", p=P))
                load(k.rb[:], a["router_b"])
                sp.wait_ge(in_rows, n_rows[0])

            @block.tensor
            def _(pe):
                pe.wait_ge(in_tables, 16)
                pe.wait_ge(in_x, 16)
                for c in range(KC):
                    for i in range(TT):
                        mm = pe.transpose(half(k.ps, c)[:, i * P:(i + 1) * P], xrow[:, i, c * P:(c + 1) * P], k.ident)
                mm.then_inc(turned, 1)
                pe.wait_ge(in_rows, n_rows[0])
                for i in range(NPT):
                    mm = pe.transpose(k.ps[:, 4 + i // 4, (i % 4) * P:(i % 4 + 1) * P], rows[:, i, :], k.ident)
                mm.then_inc(turned, 1)

            @block.scalar
            def _(act):
                act.wait_ge(turned, 1)
                act.activation(k.xT[:], place_rows(k.ps, P)[:, 0:KC], ACT.Copy).then_inc(moved, 1)
                act.wait_ge(turned, 2)
                act.activation(k.cols[:, 0:4], k.ps[:, 4, :].rearrange("p (i r) -> p i r", i=4), ACT.Copy).then_inc(moved, 1)
                act.activation(k.cols[:, 4:5], k.ps[:, 5:6, 0:P], ACT.Copy).then_inc(moved, 1)
                act.wait_ge(moved, 3)
                act.activation(k.c_act[:], k.col("c", 0, 8), ACT.Silu).then_inc(moved, 1)
                act.wait_ge(in_rows, n_rows[0])
                for e in range(2):
                    act.activation(k.cols[64 * e:64 * e + 64, 4, 88:96],
                                   skip[64 * e:64 * e + 64].rearrange("p (b e) -> p e b", e=2)[:, e], ACT.Copy).then_inc(moved, 1)
                for n, i in ((DNH, 0), (DNH, 2), (SSH, 4)):
                    act.activation(k.nega[0:n, i:i + 1], k.hp[0:n, i:i + 1], ACT.Exp).then_inc(exp_a, 1)

            @block.vector
            def _(dve):
                dve.wait_ge(exp_a, 3)
                for n, i in ((DNH, 0), (DNH, 2), (SSH, 4)):
                    ins = dve.tensor_scalar(k.nega[0:n, i:i + 1], k.nega[0:n, i:i + 1], -1.0, None, ALU.mult)
                ins.then_inc(moved, 1)


def modulation(k):
    g0 = k.start["ada0"]
    n = 12
    with ExitStack() as ctx:
        row = k.sb("mod_row", [1, L, n * 512], ctx=ctx)
        rows = k.sb("mod_rows", [48, L, P], ctx=ctx)
        with k.stage("modulation") as st:
            block = st.block
            row_moved, rows_in, turned, added, scaled = st.signals(5)

            @block.gpsimd
            def _(pool):
                st.clear_last(pool)

            @block.sync
            def _(sp):
                k.issue(sp, g0 + 2 * n + R)

            @block.tensor
            def _(pe):
                for l in range(L):
                    def panel(q, it, g=g0 + l * n, l=l):
                        s = (g + q) % R
                        pe.wait_ge(k.loaded[s], k.load_value(g + q, it))
                        pe.wait_ge(row_moved, it * R + (l * n + q + 1))
                        w = k.ring[:, s].rearrange("p (c n) -> p c n", c=KC)
                        for c in range(KC):
                            mm = pe.matmul(k.ps[0:1, s, :], k.c_act[:, c:c + 1], w[:, c], start=(c == 0), stop=(c == KC - 1))
                        mm.then_inc(k.used, 1)
                    over_rounds(pe, n, panel)
                pe.wait_ge(rows_in, 16 * L)
                for l in range(L):
                    mm = pe.transpose(k.ps[:, 4, l * 48:(l + 1) * 48], rows[:, l, :], k.ident[0:48, 0:48])
                mm.then_inc(turned, 1)

            @block.scalar
            def _(act):
                act.sem_inc(row_moved, R)
                for l in range(L):
                    def panel(q, it, g=g0 + l * n, l=l):
                        act.wait_ge(k.used, it * R + (g + q + 1))
                        act.activation(row[0:1, l, bass.ds(it * (R * 512) + q * 512, 512)], k.ps[0:1, (g + q) % R, :],
                                       ACT.Copy).then_inc(row_moved, 1)
                    over_rounds(act, n, panel)
                    act.wait_ge(row_moved, R + (l + 1) * n)
                    act.dma_start(rows[:, l, :], row[0:1, l, :].rearrange("o (r p) -> o r p", p=P)).then_inc(rows_in, 16)

            @block.vector
            def _(dve):
                dve.wait_ge(turned, 1)
                for l in range(L):
                    dve.tensor_tensor(k.mod[:, l], k.ps[:, 4, l * 48:(l + 1) * 48], k.col(f"ada_b{l}", 0, 48),
                                      ALU.add).then_inc(added, 1)
                dve.wait_ge(added, L)
                for l in range(L):
                    for j, w in ((1, "norm_mix"), (4, "norm_ffn")):
                        sc = k.mod[:, l, 8 * j:8 * j + 8]
                        dve.scalar_tensor_tensor(sc, sc, 1.0, k.col(f"{w}{l}", 0, 8), ALU.add, ALU.mult).then_inc(scaled, 1)


def rms(k, name, src, out, scale, shift=None, upto=0):
    with ExitStack() as ctx:
        sq = k.sb(f"sq_{name}", [P, KC, T], ctx=ctx)
        rs = k.sb(f"rs_{name}", [P, T], ctx=ctx)
        with k.stage(name) as st:
            block = st.block
            squared, summed, mean, root, chain, done = st.signals(6)

            @block.gpsimd
            def _(pool):
                st.clear_last(pool)

            @block.scalar
            def _(act):
                for c in range(0, KC, 2):
                    act.activation(sq[:, c:c + 2], src[:, c:c + 2], ACT.Square).then_inc(squared, 1)
                act.wait_ge(mean, 1)
                act.activation(rs[:], rs[:], ACT.Sqrt).then_inc(root, 1)

            @block.tensor
            def _(pe):
                for c in range(KC):
                    pe.wait_ge(squared, c // 2 + 1)
                    mm = pe.matmul(half(k.ps, 0), k.ones, sq[:, c], start=(c == 0), stop=(c == KC - 1))
                mm.then_inc(summed, 1)

            @block.vector
            def _(dve):
                link = Chain(dve, chain)
                dve.wait_ge(summed, 1)
                dve.tensor_scalar(rs[:], half(k.ps, 0), 1.0 / D, EPS, ALU.mult, ALU.add).then_inc(mean, 1)
                dve.wait_ge(root, 1)
                link(dve.reciprocal(rs[:], rs[:]))
                link(dve.tensor_tensor(out[:], src[:], row_bc(rs[:], KC), ALU.mult))
                for c in range(KC):
                    if shift is None:
                        dve.tensor_scalar(out[:, c], out[:, c], scale[:, c:c + 1], None, ALU.mult).then_inc(done, 1)
                    else:
                        dve.tensor_scalar(out[:, c], out[:, c], scale[:, c:c + 1], shift[:, c:c + 1],
                                          ALU.mult, ALU.add).then_inc(done, 1)


def head_gates(k, name, w, n, ia, cols_g, rows_g, cols_b=None, rows_b=None, whole=False, out_b=None, keep=None):
    with ExitStack() as ctx:
        z = k.sb(f"z_{name}", [SSH, T], ctx=ctx)
        sp_ = k.sb(f"softplus_{name}", [SSH, T], ctx=ctx)
        g = keep if keep is not None else k.sb(f"g_{name}", [SSH, T], ctx=ctx)
        beta = k.sb(f"beta_{name}", [SSH, T], ctx=ctx)
        one = k.sb(f"one_{name}", [SSH, T], ctx=ctx)
        with k.stage(name) as st:
            block = st.block
            projected, biased, act_chain, logged, dve_chain, sums, turned, turned_out, spread, moved, has_beta = st.signals(11)
            h = k.h
            a0 = n if rows_b is not None else 0
            made = [(g, cols_g, rows_g)] + ([(beta, cols_b, rows_b)] if rows_b is not None else [(sp_, out_b, None)])
            rowed = [(m, r) for m, _, r in made if r is not None]

            @block.gpsimd
            def _(pool):
                st.clear_last(pool)

            @block.tensor
            def _(pe):
                for m, first in enumerate((a0, 0) if rows_b is not None else (0,)):
                    for c in range(KC):
                        mm = pe.matmul(half(k.ps, 2 * m)[0:n], w[:, c, first:first + n], h[:, c], start=(c == 0), stop=(c == KC - 1))
                    mm.then_inc(projected, 1)
                pe.wait_ge(sums, 1)
                if rows_b is not None:
                    pe.wait_ge(has_beta, 1)
                for m, (tile, _, _) in enumerate(made):
                    for i in range(TT):
                        mm = pe.transpose(k.ps[:, 2, (2 * m + i) * n:(2 * m + i + 1) * n], tile[0:n, i * P:(i + 1) * P], k.ident[0:n, 0:n])
                mm.then_inc(turned, 1)
                pe.wait_ge(turned_out, 2)
                done = 0
                for m, (tile, _) in enumerate(rowed):
                    for hh in range(0, n, 4):
                        if done >= 2:
                            pe.wait_ge(moved, done - 1)
                        for e in range(4):
                            mm = pe.matmul(half(k.ps, 8 + 4 * (done % 2) + e), k.ident[0:n, hh + e:hh + e + 1].to_broadcast([n, P]),
                                           tile[0:n, :], start=True, stop=True)
                        mm.then_inc(spread, 1)
                        done += 1

            @block.vector
            def _(dve):
                link = Chain(dve, dve_chain)
                link(dve.memset(one[:], 1.0))
                dve.wait_ge(projected, 1)
                dve.tensor_scalar(z[0:n], half(k.ps, 0)[0:n], k.hp[0:n, ia + 1:ia + 2], None, ALU.add).then_inc(biased, 1)
                dve.wait_ge(logged, 1)
                link(dve.scalar_tensor_tensor(sp_[0:n], z[0:n], 0.0, sp_[0:n], ALU.max, ALU.add))
                link(dve.tensor_scalar(z[0:n], sp_[0:n], k.nega[0:n, ia:ia + 1], None, ALU.mult))
                if whole:
                    dve.tensor_tensor_scan(g[0:n], one[0:n], z[0:n], 0.0, ALU.mult, ALU.add).then_inc(sums, 1)
                else:
                    for i in range(TT):
                        ts = slice(i * P, (i + 1) * P)
                        ins = dve.tensor_tensor_scan(g[0:n, ts], one[0:n, ts], z[0:n, ts], 0.0, ALU.mult, ALU.add)
                    ins.then_inc(sums, 1)
                dve.wait_ge(turned, 1)
                for m, (_, cols, _) in enumerate(made):
                    dve.tensor_copy(cols[:], k.ps[:, 2, 2 * m * n:(2 * m + 2) * n].rearrange("p (i h) -> p i h", i=TT)).then_inc(turned_out, 1)

            @block.scalar
            def _(act):
                act.wait_ge(biased, 1)
                link = Chain(act, act_chain)
                link(act.activation(sp_[0:n], z[0:n], ACT.Abs))
                link(act.activation(sp_[0:n], sp_[0:n], ACT.Exp, scale=-1.0))
                act.activation(sp_[0:n], sp_[0:n], ACT.Ln, bias=1.0).then_inc(logged, 1)
                if rows_b is not None:
                    act.wait_ge(projected, 2)
                    act.activation(beta[0:n], half(k.ps, 2)[0:n], ACT.Sigmoid).then_inc(has_beta, 1)
                done = 0
                for m, (_, rows) in enumerate(rowed):
                    for hh in range(0, n, 4):
                        act.wait_ge(spread, done + 1)
                        act.activation(rows[:, hh:hh + 4], place_rows(k.ps, P)[:, 8 + 4 * (done % 2):12 + 4 * (done % 2)], ACT.Copy).then_inc(moved, 1)
                        done += 1


def conv_silu(k, name, blk0, n, conv, bias=None):
    with ExitStack() as ctx:
        tmp = k.sb(f"tmp_{name}", [P, 2, T], ctx=ctx)
        with k.stage(name) as st:
            block = st.block
            tmp_free, step, tmp_ready = st.signals(3)
            tile, r0 = k.col_at[conv]

            @block.gpsimd
            def _(pool):
                st.clear_last(pool)

            @block.vector
            def _(dve):
                with dve.Fori(0, n // 2) as it:
                    for q in range(2):
                        x = k.proj[:, bass.ds(it * 2 + (blk0 + q), 1)]
                        y = tmp[:, q:q + 1]

                        def tap(j, q=q, it=it):
                            return k.cols[:, tile, bass.ds(it * 2 + (r0 + j * n + q), 1)]
                        dve.wait_ge(tmp_free, it * 2 + (q + 1))
                        dve.tensor_scalar(y, x, tap(3), None, ALU.mult).then_inc(step, 1)
                        for s in range(1, 4):
                            dve.wait_ge(step, it * 6 + (3 * q + s))
                            dve.scalar_tensor_tensor(y[:, :, s:T], x[:, :, 0:T - s], tap(3 - s), y[:, :, s:T],
                                                     ALU.mult, ALU.add).then_inc(step if s < 3 else tmp_ready, 1)

            @block.scalar
            def _(act):
                act.sem_inc(tmp_free, 2)
                with act.Fori(0, n // 2) as it:
                    for q in range(2):
                        act.wait_ge(tmp_ready, it * 2 + (q + 1))
                        b = 0.0 if bias is None else k.cols[:, k.col_at[bias][0], bass.ds(it * 2 + (k.col_at[bias][1] + q), 1)]
                        act.activation(k.proj[:, bass.ds(it * 2 + (blk0 + q), 1)], tmp[:, q:q + 1], ACT.Silu, bias=b).then_inc(tmp_free, 1)


def unit_rows(k, name, specs, ones):
    with ExitStack() as ctx:
        sq = k.sb(f"sq_{name}", [P, 8, T], ctx=ctx)
        with k.stage(name) as st:
            block = st.block
            squared, summed, mean, root, chain, done = st.signals(6)

            @block.gpsimd
            def _(pool):
                st.clear_last(pool)

            @block.scalar
            def _(act):
                for i, (b0, n, factor, eps, w) in enumerate(specs):
                    if i:
                        act.wait_ge(done, i)
                    act.activation(sq[:, 0:n], k.proj[:, b0:b0 + n], ACT.Square).then_inc(squared, 1)
                    act.wait_ge(mean, i + 1)
                    act.activation(sq[:, 0:n], sq[:, 0:n], ACT.Sqrt).then_inc(root, 1)

            @block.tensor
            def _(pe):
                for i, (b0, n, factor, eps, w) in enumerate(specs):
                    pe.wait_ge(squared, i + 1)
                    for c in range(0, n, 2):
                        mm = pe.matmul(k.ps[:, c // 2, :], ones, sq[:, c:c + 2], start=True, stop=True)
                    mm.then_inc(summed, 1)

            @block.vector
            def _(dve):
                link = Chain(dve, chain)
                for i, (b0, n, factor, eps, w) in enumerate(specs):
                    dve.wait_ge(summed, i + 1)
                    dve.tensor_scalar(sq[:, 0:n], place_rows(k.ps, P)[:, 0:n], factor, eps, ALU.mult, ALU.add).then_inc(mean, 1)
                    dve.wait_ge(root, i + 1)
                    link(dve.reciprocal(sq[:, 0:n], sq[:, 0:n]))
                    x = k.proj[:, b0:b0 + n]
                    if w is None:
                        dve.tensor_tensor(x, x, sq[:, 0:n], ALU.mult).then_inc(done, 1)
                    else:
                        dve.scalar_tensor_tensor(x, x, w, sq[:, 0:n], ALU.mult, ALU.mult).then_inc(done, 1)


def delta_rule(k, l):
    H = DNH
    SYS = [(c, hh) for c in range(TT) for hh in (0, 4)]
    with ExitStack() as ctx:
        gcol = k.sb(f"gcol{l}", [P, TT, H], ctx=ctx)
        bcol = k.sb(f"bcol{l}", [P, TT, H], ctx=ctx)
        grow = k.sb(f"grow{l}", [P, H, T], ctx=ctx)
        brow = k.sb(f"brow{l}", [P, H, T], ctx=ctx)
        head_gates(k, f"delta_gates{l}", k.wba[:, l], H, 2 * l, gcol, grow, bcol, brow)
        conv_silu(k, f"delta_conv{l}", Q0, 24, f"conv{l}")
        unit_rows(k, f"delta_unit{l}", [(Q0, 8, float(P), EPS * P, None), (K0, 8, 1.0, EPS, None)], k.ones)

        decay = k.sb(f"decay{l}", [P, 4, 4, P], ctx=ctx)
        lower = k.sb(f"lower{l}", [P, 4, 4, P], ctx=ctx)
        xi = k.h.rearrange("p b (j t) -> p (b j) t", j=2).rearrange("p (g e) t -> p g e t", g=4)
        xt = k.sb(f"invT{l}", [P, 4, 4, P], ctx=ctx)
        vb = k.o[:, 8:16].rearrange("p b (j t) -> p (b j) t", j=2).rearrange("p (g e) t -> p g e t", g=4)
        kb = k.sb(f"k_beta{l}", [P, 2, 4, P], ctx=ctx)
        kd = k.sb(f"k_decay{l}", [P, 2, 4, P], ctx=ctx)
        fac = k.sb(f"factors{l}", [P, 2, H], ctx=ctx)
        level = k.sb(f"levels{l}", [P, 7, P], ctx=ctx)
        with k.stage(f"delta_products{l}") as st:
            block = st.block
            turned, taken, multiplied, spread, decayed, chain, facs, facs_e, in_level, ends = st.signals(10)

            @block.gpsimd
            def _(pool):
                st.clear_last(pool)

            @block.sync
            def _(sp):
                sp.dma_start(level[:], k.a["table_level"].rearrange("p (n t) -> p n t", n=7)).then_inc(in_level, 16)
                sp.wait_ge(in_level, 16)

            @block.tensor
            def _(pe):
                for b0, bank0 in ((V0, 4), (K0, 0)):
                    for g, (c, hh) in enumerate(SYS):
                        for e in range(4):
                            mm = pe.transpose(k.ps[:, bank0 + g, e * P:(e + 1) * P], k.proj[:, b0 + hh + e, c * P:(c + 1) * P], k.ident)
                        mm.then_inc(turned, 1)
                pe.wait_ge(taken, 8)
                for g, (c, hh) in enumerate(SYS):
                    ts = slice(c * P, (c + 1) * P)
                    for rhs0, bank0 in ((K0, 0), (Q0, 4)):
                        for e in range(4):
                            mm = pe.matmul(k.ps[:, bank0 + g, e * P:(e + 1) * P], k.proj[:, K0 + hh + e, ts],
                                           k.proj[:, rhs0 + hh + e, ts], start=True, stop=True)
                    mm.then_inc(multiplied, 1)

            @block.vector
            def _(dve):
                link = Chain(dve, chain)
                link(dve.tensor_copy(fac[:, 1], gcol[:, 1]))
                link(dve.tensor_copy(fac[:, 0], grow[:, :, P - 1]))
                dve.tensor_tensor(fac[:, 0], fac[:, 0], gcol[:, 0], ALU.subtract).then_inc(facs, 1)
                for g, (c, hh) in enumerate(SYS):
                    for e in range(4):
                        dve.scalar_tensor_tensor(decay[:, g, e], grow[:, hh + e, c * P:(c + 1) * P], gcol[:, c, hh + e:hh + e + 1],
                                                 k.neg_le, ALU.subtract, ALU.add).then_inc(spread, 1)
                dve.wait_ge(facs_e, 2)
                link(dve.tensor_tensor(fac[:, 1], fac[:, 1], bcol[:, 1], ALU.mult))
                for g, (c, hh) in enumerate(SYS):
                    dve.wait_ge(turned, g + 1)
                    dve.tensor_tensor(vb[:, g], k.ps[:, 4 + g, :].rearrange("p (e d) -> p e d", e=4), col_bc(bcol[:, c, hh:hh + 4], P), ALU.mult).then_inc(taken, 1)
                for g, (c, hh) in enumerate(SYS):
                    dve.wait_ge(turned, 4 + g + 1)
                    out = kd[:, g] if c == 0 else kb[:, g - 2]
                    dve.tensor_tensor(out, k.ps[:, g, :].rearrange("p (e d) -> p e d", e=4), col_bc(fac[:, c, hh:hh + 4], P), ALU.mult).then_inc(taken, 1)
                for g, (c, hh) in enumerate(SYS):
                    dve.wait_ge(decayed, g + 1)
                    dve.wait_ge(multiplied, g + 1)
                    link(dve.tensor_tensor(lower[:, g], k.ps[:, g, :].rearrange("p (e t) -> p e t", e=4), decay[:, g], ALU.mult))
                    link(dve.tensor_tensor(lower[:, g], lower[:, g], brow[:, hh:hh + 4, c * P:(c + 1) * P], ALU.mult))
                    link(dve.tensor_tensor(decay[:, g], k.ps[:, 4 + g, :].rearrange("p (e t) -> p e t", e=4), decay[:, g], ALU.mult))
                dve.wait_ge(ends, 1)
                q1 = k.proj[:, Q0:Q0 + 8, P:T]
                link(dve.tensor_tensor(q1, q1, grow[:, :, P:T], ALU.mult))

            @block.scalar
            def _(act):
                act.wait_ge(facs, 1)
                for c in range(2):
                    act.activation(fac[:, c], fac[:, c], ACT.Exp).then_inc(facs_e, 1)
                for g in range(4):
                    act.wait_ge(spread, 4 * g + 4)
                    act.activation(decay[:, g], decay[:, g], ACT.Exp).then_inc(decayed, 1)
                act.activation(grow[:, :, P:T], grow[:, :, P:T], ACT.Exp).then_inc(ends, 1)

        mt = k.proj[:, V0:V0 + 8].rearrange("p b (j t) -> p (b j) t", j=2).rearrange("p (g e) t -> p g e t", g=4)
        px = k.proj[:, K0:K0 + 8].rearrange("p b (j t) -> p (b j) t", j=2).rearrange("p (g e) t -> p g e t", g=4)
        with k.stage(f"delta_inverse{l}") as st:
            block = st.block
            started, masked, right, copied, both, updated = st.signals(6)

            def bank(b):
                return k.ps[:, b, :].rearrange("p (e t) -> p e t", e=4)

            @block.gpsimd
            def _(pool):
                st.clear_last(pool)

            @block.vector
            def _(dve):
                for g in range(4):
                    for x in (xi, xt):
                        dve.tensor_copy(x[:, g], row_bc(k.ident, 4)).then_inc(started, 1)
                def mask(n):
                    if n >= 4:
                        dve.wait_ge(right, n - 4 + 1)
                    dve.tensor_tensor(mt[:, n % 4], lower[:, n % 4], row_bc(level[:, n // 4], 4), ALU.mult).then_inc(masked, 1)
                for n in range(4):
                    mask(n)
                dve.wait_ge(started, 8)
                for n in range(28):
                    g = n % 4
                    dve.wait_ge(both, n + 1)
                    if n >= 4:
                        dve.wait_ge(updated, 2 * n - 8 + 2)
                    b = 2 + 2 * (g % 2)
                    dve.tensor_tensor(xi[:, g], xi[:, g], bank(b), ALU.subtract).then_inc(updated, 1)
                    dve.tensor_tensor(xt[:, g], xt[:, g], bank(b + 1), ALU.subtract).then_inc(updated, 1)
                    if n + 4 < 28:
                        mask(n + 4)

            @block.tensor
            def _(pe):
                pe.wait_ge(started, 8)

                def right_product(n):
                    g = n % 4
                    pe.wait_ge(masked, n + 1)
                    if n >= 4:
                        pe.wait_ge(updated, 2 * (n - 4) + 2)
                    if n >= 2:
                        pe.wait_ge(copied, n - 1)
                    for e in range(4):
                        mm = pe.matmul(bank(g % 2)[:, e], mt[:, g, e], xi[:, g, e], start=True, stop=True)
                    mm.then_inc(right, 1)

                def both_products(n):
                    g = n % 4
                    pe.wait_ge(copied, n + 1)
                    if n >= 2:
                        pe.wait_ge(updated, 2 * (n - 2) + 2)
                    b = 2 + 2 * (g % 2)
                    for e in range(4):
                        pe.matmul(bank(b)[:, e], xt[:, g, e], px[:, g, e], start=True, stop=True)
                    for e in range(4):
                        mm = pe.matmul(bank(b + 1)[:, e], px[:, g, e], xt[:, g, e], start=True, stop=True)
                    mm.then_inc(both, 1)
                for n in range(28 + 1):
                    if n < 28:
                        right_product(n)
                    if n >= 1:
                        both_products(n - 1)

            @block.scalar
            def _(act):
                for n in range(28):
                    act.wait_ge(right, n + 1)
                    if n >= 4:
                        act.wait_ge(both, n - 4 + 1)
                    act.activation(px[:, n % 4], bank(n % 2), ACT.Copy).then_inc(copied, 1)

        v0 = brow[:].rearrange("p h (j t) -> p (h j) t", j=2).rearrange("p (c g e) t -> p c g e t", c=2, g=2)
        s1 = xi[:, 0:2]
        nw = xi[:, 2:4]
        with k.stage(f"delta_outputs{l}") as st:
            block = st.block
            first, first_out, second, second_out, third, third_out, fourth = st.signals(7)

            def banks(b):
                return k.ps[:, b:b + 2, :].rearrange("p g (e t) -> p g e t", e=4)

            @block.gpsimd
            def _(pool):
                st.clear_last(pool)

            @block.tensor
            def _(pe):
                def each(b, lhs, rhs, more=None):
                    for g in range(2):
                        for e in range(4):
                            mm = pe.matmul(banks(b)[:, g, e], lhs(g, e), rhs(g, e), start=True, stop=more is None)
                            if more:
                                mm = pe.matmul(banks(b)[:, g, e], more[0](g, e), more[1](g, e), start=False, stop=True)
                    return mm
                each(0, lambda g, e: xt[:, g, e], lambda g, e: vb[:, g, e]).then_inc(first, 1)
                each(2, lambda g, e: kb[:, g, e], lambda g, e: xt[:, 2 + g, e]).then_inc(first, 1)
                pe.wait_ge(first_out, 1)
                each(4, lambda g, e: kd[:, g, e], lambda g, e: v0[:, 0, g, e]).then_inc(second, 1)
                each(6, lambda g, e: v0[:, 0, g, e], lambda g, e: decay[:, g, e]).then_inc(second, 1)
                pe.wait_ge(first_out, 2)
                pe.wait_ge(second_out, 1)
                each(0, lambda g, e: xt[:, 2 + g, e], lambda g, e: vb[:, 2 + g, e],
                     (lambda g, e: nw[:, g, e], lambda g, e: s1[:, g, e])).then_inc(third, 1)
                pe.wait_ge(third_out, 1)
                each(2, lambda g, e: v0[:, 1, g, e], lambda g, e: decay[:, 2 + g, e],
                     (lambda g, e: s1[:, g, e], lambda g, e: k.proj[:, Q0 + 4 * g + e, P:T])).then_inc(fourth, 1)

            o4 = k.o[:, 0:8].rearrange("p (g e) t -> p g e t", g=2)

            @block.scalar
            def _(act):
                act.wait_ge(first, 1)
                act.activation(v0[:, 0], banks(0), ACT.Copy).then_inc(first_out, 1)
                act.wait_ge(first, 2)
                act.activation(nw, banks(2), ACT.Copy, scale=-1.0).then_inc(first_out, 1)
                act.wait_ge(second, 1)
                act.activation(s1, banks(4), ACT.Copy).then_inc(second_out, 1)
                act.wait_ge(third, 1)
                act.activation(v0[:, 1], banks(0), ACT.Copy).then_inc(third_out, 1)
                act.wait_ge(second, 2)
                act.activation(o4[:, :, :, 0:P], banks(6), ACT.Copy).then_inc(second_out, 1)
                act.wait_ge(fourth, 1)
                act.activation(o4[:, :, :, P:T], banks(2), ACT.Copy).then_inc(third_out, 1)

    with ExitStack() as ctx:
        sq = k.sb(f"sq_out{l}", [P, 8, T], ctx=ctx)
        with k.stage(f"delta_norm{l}") as st:
            block = st.block
            squared, summed, mean, root, chain = st.signals(5)
            z = k.proj[:, Z0:Z0 + 8]

            @block.gpsimd
            def _(pool):
                st.clear_last(pool)

            @block.scalar
            def _(act):
                act.activation(sq[:], k.o[:, 0:8], ACT.Square).then_inc(squared, 1)
                act.activation(z, z, ACT.Silu).then_inc(squared, 1)
                act.wait_ge(mean, 1)
                act.activation(sq[:], sq[:], ACT.Sqrt).then_inc(root, 1)

            @block.tensor
            def _(pe):
                pe.wait_ge(squared, 1)
                for c in range(4):
                    mm = pe.matmul(k.ps[:, c, :], k.ones, sq[:, 2 * c:2 * c + 2], start=True, stop=True)
                mm.then_inc(summed, 1)

            @block.vector
            def _(dve):
                link = Chain(dve, chain)
                dve.wait_ge(summed, 1)
                dve.tensor_scalar(sq[:], place_rows(k.ps, P)[:, 0:8], 1.0 / P, EPS, ALU.mult, ALU.add).then_inc(mean, 1)
                dve.wait_ge(root, 1)
                link(dve.reciprocal(sq[:], sq[:]))
                o = k.o[:, 0:8]
                link(dve.scalar_tensor_tensor(o, o, k.col(f"out_norm{l}", 0, 1), sq[:], ALU.mult, ALU.mult))
                dve.wait_ge(squared, 2)
                link(dve.tensor_tensor(o, o, z, ALU.mult))


def to_tokens(k, name, blk0, n, out):
    with k.stage(name) as st:
        turned, moved = st.signals(2)
        block = st.block

        @block.gpsimd
        def _(pool):
            st.clear_last(pool)

        @block.tensor
        def _(pe):
            for b in range(n):
                for i in range(TT):
                    mm = pe.transpose(place_rows(k.ps, P)[:, b, i * P:(i + 1) * P], k.proj[:, blk0 + b, i * P:(i + 1) * P], k.ident)
                mm.then_inc(turned, 1)

        @block.scalar
        def _(act):
            act.wait_ge(turned, n)
            for i in range(TT):
                act.activation(out[:, i].rearrange("p (b d) -> p b d", b=n), place_rows(k.ps, P)[:, 0:n, i * P:(i + 1) * P], ACT.Copy).then_inc(moved, 1)


def stick_breaking(k, l):
    W = T + P
    with ExitStack() as ctx:
        vt = k.sb(f"sb_v{l}", [P, TT, 4 * P], ctx=ctx)
        to_tokens(k, f"sb_turn{l}", SV0, 4, vt)
        z = k.sb(f"sb_z{l}", [P, 4, W], ctx=ctx)
        e = k.sb(f"sb_e{l}", [P, 4, W], ctx=ctx)
        at = k.sb(f"sb_att{l}", [P, 2, W], ctx=ctx)
        with k.stage(f"sb_heads{l}") as st:
            block = st.block
            scored, z_ready, act_chain, logged, dve_chain, summed_in, summed, shifted, attn, out_ready, out_taken = st.signals(11)
            H = SBH

            def diag(t):
                return t.rearrange("p (i t) -> p i t", i=3)[:, 0:3:2, :]

            @block.gpsimd
            def _(pool):
                st.clear_last(pool)

            @block.tensor
            def _(pe):
                def score(h):
                    if h >= 2:
                        pe.wait_ge(z_ready, h - 1)
                    rows, b = slice(64 * (h % 2), 64 * (h % 2) + 64), h // 2
                    pe.matmul(k.ps[:, h % 2, 0:T], k.proj[rows, SK0 + b, 0:P], k.proj[rows, SQ0 + b, :], start=True, stop=True)
                    pe.matmul(k.ps[:, h % 2, T:W], k.proj[rows, SK0 + b, P:T], k.proj[rows, SQ0 + b, P:T], start=True, stop=True).then_inc(scored, 1)

                def later(h):
                    pe.wait_ge(summed_in, h + 1)
                    if h >= 2:
                        pe.wait_ge(shifted, h - 1)
                    o = k.ps[:, 2 + h % 2, :]
                    s = e[:, h % 4]
                    pe.matmul(o[:, 0:T], k.tri_ge, s[:, 0:T], start=True, stop=False, skip_group_check=True)
                    pe.matmul(o[:, P:T], k.ones, s[:, T:W], start=False, stop=True, skip_group_check=True)
                    pe.matmul(o[:, T:W], k.tri_ge, s[:, T:W], start=True, stop=True, skip_group_check=True).then_inc(summed, 1)

                def mix(h):
                    pe.wait_ge(attn, h + 1)
                    if h >= 4 and h % 2 == 0:
                        pe.wait_ge(out_taken, h // 2 - 1)
                    r0 = 64 * (h % 2)
                    o = k.ps[r0:r0 + 64, 4 + (h // 2) % 2, :]
                    pe.matmul(o[:, 0:T], vt[:, 0, 64 * h:64 * h + 64], at[:, h % 2, 0:T], start=True, stop=False, skip_group_check=True)
                    pe.matmul(o[:, P:T], vt[:, 1, 64 * h:64 * h + 64], at[:, h % 2, T:W], start=False, stop=True, skip_group_check=True).then_inc(out_ready, 1)
                for i in range(H + 3):
                    if i < H:
                        score(i)
                    if 0 <= i - 2 < H:
                        later(i - 2)
                    if 0 <= i - 3 < H:
                        mix(i - 3)

            @block.vector
            def _(dve):
                link = Chain(dve, dve_chain)

                def first(h):
                    dve.wait_ge(scored, h + 1)
                    dve.tensor_scalar(z[:, h % 4], k.ps[:, h % 2, 0:W], 64 ** -0.5, None, ALU.mult).then_inc(z_ready, 1)

                def second(h):
                    dve.wait_ge(logged, h + 1)
                    s = e[:, h % 4]
                    link(dve.scalar_tensor_tensor(s, z[:, h % 4], 0.0, s, ALU.max, ALU.add))
                    dve.tensor_tensor(diag(s), diag(s), row_bc(k.msk_lt, 2), ALU.mult).then_inc(summed_in, 1)

                def third(h):
                    dve.wait_ge(summed, h + 1)
                    zz = z[:, h % 4]
                    link(dve.tensor_tensor(zz, zz, k.ps[:, 2 + h % 2, 0:W], ALU.subtract))
                    dve.tensor_tensor(diag(zz), diag(zz), row_bc(k.neg_lt, 2), ALU.add).then_inc(shifted, 1)
                for i in range(H + 2):
                    if i < H:
                        first(i)
                    if 0 <= i - 1 < H:
                        second(i - 1)
                    if 0 <= i - 2 < H:
                        third(i - 2)

            @block.scalar
            def _(act):
                link = Chain(act, act_chain)

                def soft(h):
                    act.wait_ge(z_ready, h + 1)
                    if h >= 4:
                        act.wait_ge(summed, h - 3)
                    s = e[:, h % 4]
                    link(act.activation(s, z[:, h % 4], ACT.Abs))
                    link(act.activation(s, s, ACT.Exp, scale=-1.0))
                    act.activation(s, s, ACT.Ln, bias=1.0).then_inc(logged, 1)

                def weight(h):
                    act.wait_ge(shifted, h + 1)
                    if h >= 2:
                        act.wait_ge(out_ready, h - 1)
                    act.activation(at[:, h % 2], z[:, h % 4], ACT.Exp).then_inc(attn, 1)

                def take(b):
                    act.wait_ge(out_ready, 2 * b + 2)
                    act.activation(k.o[:, 8 + b], k.ps[:, 4 + b % 2, 0:T], ACT.Copy).then_inc(out_taken, 1)
                for i in range(H + 4):
                    if i < H:
                        soft(i)
                    if 0 <= i - 2 < H:
                        weight(i - 2)
                    if i >= 4 and (i - 4) % 2 == 1:
                        take((i - 4) // 2)


def branches(k, name, parts, gates, wout, gate):
    n_all = sum(len(p) for p, _ in parts) + 2
    first = parts[0][0][0][0]
    with ExitStack() as ctx:
        merged = k.sb(f"merged_{name}", [P, KC, T], ctx=ctx)
        tmp = k.sb(f"tmp_{name}", [P, KC, T], ctx=ctx)
        with k.stage(name) as st:
            block = st.block
            opened, made, taken, chain, out_made, out_taken = st.signals(6)

            @block.gpsimd
            def _(pool):
                st.clear_last(pool)

            @block.sync
            def _(sp):
                k.issue(sp, first + n_all + R)

            def gate_of(i):
                return k.proj[:, gates[i]:gates[i] + 8]

            @block.scalar
            def _(act):
                for i in range(len(parts)):
                    act.activation(gate_of(i), gate_of(i), ACT.Sigmoid).then_inc(opened, 1)

            def place(i, j):
                return half(k.ps, 8 * (i % 2) + j)

            @block.tensor
            def _(pe):
                for i, (panels, src0) in enumerate(parts):
                    if i >= 2:
                        pe.wait_ge(taken, i - 1)
                    wide = panels[0][1]
                    if wide:
                        total = sum(p[1] for p in panels)
                        if total > 4 or len(panels) > 1:
                            for g, kb in panels:
                                pe.wait_ge(k.loaded[g % R], k.value[g])
                        else:
                            pe.wait_ge(k.loaded[panels[0][0] % R], k.value[panels[0][0]])
                        for j in range(KC):
                            kdone = 0
                            for g, kb in panels:
                                w = k.ring[:, g % R, 0:kb * D].rearrange("p (c n) -> p c n", c=kb)
                                for c in range(kb):
                                    mm = pe.matmul(place(i, j), w[:, c, j * P:(j + 1) * P], k.o[:, src0 + kdone],
                                                   start=(kdone == 0), stop=(kdone == total - 1))
                                    kdone += 1
                        mm.then_inc(k.used, len(panels))
                    else:
                        for m, (g, _) in enumerate(panels):
                            pe.wait_ge(k.loaded[g % R], k.value[g])
                            w = k.ring[:, g % R].rearrange("p (c n) -> p c n", c=KC)
                            for j in range(4):
                                for c in range(KC):
                                    mm = pe.matmul(place(i, 4 * m + j), w[:, c, j * P:(j + 1) * P], k.o[:, src0 + c],
                                                   start=(c == 0), stop=(c == KC - 1))
                            mm.then_inc(k.used, 1)
                pe.wait_ge(taken, len(parts))
                for m in range(2):
                    g = wout + m
                    pe.wait_ge(k.loaded[g % R], k.value[g])
                    w = k.ring[:, g % R].rearrange("p (c n) -> p c n", c=KC)
                    for j in range(4):
                        for c in range(KC):
                            mm = pe.matmul(place(len(parts), 4 * m + j), w[:, c, j * P:(j + 1) * P], merged[:, c],
                                           start=(c == 0), stop=(c == KC - 1))
                    mm.then_inc(k.used, 1)

            @block.vector
            def _(dve):
                link = Chain(dve, chain)
                n_used = first
                for i, (panels, _) in enumerate(parts):
                    n_used += len(panels)
                    dve.wait_ge(k.used, n_used)
                    dve.wait_ge(opened, i + 1)
                    ps = place_rows(k.ps, P)[:, 8 * (i % 2):8 * (i % 2) + 8]
                    if i == 0:
                        dve.tensor_tensor(merged[:], ps, gate_of(i), ALU.mult).then_inc(taken, 1)
                    else:
                        dve.wait_ge(taken, i)
                        link(dve.tensor_tensor(tmp[:], ps, gate_of(i), ALU.mult))
                        dve.tensor_tensor(merged[:], merged[:], tmp[:], ALU.add).then_inc(taken, 1)
                for j in range(KC):
                    dve.wait_ge(k.used, n_used + 1 + j // 4)
                    ps = place(len(parts), j)
                    if gate is None:
                        link(dve.tensor_tensor(k.xT[:, j], k.xT[:, j], ps, ALU.add))
                    else:
                        link(dve.scalar_tensor_tensor(k.xT[:, j], ps, gate[:, j:j + 1], k.xT[:, j], ALU.mult, ALU.add))


class DenseSwiglu:

    def __init__(self, k, g0, tiles, signals, up_used, down_used, hidden_free, weight=None):
        self.k, self.g0, self.weight = k, g0, weight
        self.silu, self.hid, self.zero = tiles
        self.up, self.hidden, self.silued, self.weighed = signals
        self.up_used, self.down_used, self.hidden_free = up_used, down_used, hidden_free
        self.acc = [half(k.ps, 8 + j) for j in range(KC)]

    def bound(self, pe, first):
        for b in range(4):
            mm = pe.matmul(self.k.ps[:, 4 + b, :], self.zero[:, 0:P], self.zero[:], start=first, stop=not first,
                           skip_group_check=True)
        return mm

    def products(self, pe, it):
        k, g0 = self.k, self.g0
        for q in range(2):
            pe.wait_ge(k.loaded[(g0 + q) % R], k.load_value(g0 + q, it))
        w = [k.ring[:, (g0 + q) % R].rearrange("p (c n) -> p c n", c=KC) for q in range(2)]
        for j in range(4):
            for q in range(2):
                for c in range(KC):
                    mm = pe.matmul(half(k.ps, 2 * j + q), w[q][:, c, j * P:(j + 1) * P], k.h[:, c],
                                   start=(c == 0), stop=(c == KC - 1))
            mm.then_inc(self.up, 1)
        pe.wait_ge(k.loaded[(g0 + 2) % R], k.load_value(g0 + 2, it))
        w2 = k.ring[:, (g0 + 2) % R].rearrange("p (b n) -> p b n", b=4)
        for j in range(4):
            pe.wait_ge(self.hidden, it * 4 + (j + 2))
            for d in range(KC):
                mm = pe.matmul(self.acc[d], w2[:, j, d * P:(d + 1) * P], self.hid[:, j], start=False, stop=False,
                               skip_group_check=True)
        mm.then_inc(self.down_used, 1)

    def silus(self, act, it):
        for j in range(4):
            act.wait_ge(self.up, it * 4 + (j + 1))
            act.wait_ge(self.hidden, it * 4 + (j + 1))
            act.activation(self.silu[:, j:j + 1], half(self.k.ps, 2 * j).unsqueeze(1), ACT.Silu).then_inc(self.silued, 1)

    def gates(self, dve, e, it):
        for j in range(4):
            s, o, up3 = self.silu[:, j:j + 1], self.hid[:, j:j + 1], half(self.k.ps, 2 * j + 1).unsqueeze(1)
            dve.wait_ge(self.silued, it * 4 + (j + 1))
            if j == 3:
                dve.sem_inc(self.up_used, 2)
            self.hidden_free(dve, it)
            if self.weight is None:
                dve.tensor_tensor(o, s, up3, ALU.mult).then_inc(self.hidden, 1)
            else:
                dve.tensor_tensor(s, s, up3, ALU.mult).then_inc(self.weighed, 1)
                dve.wait_ge(self.weighed, it * 4 + (j + 1))
                dve.tensor_tensor(o, s, self.weight[:, bass.ds(e, 1)], ALU.mult).then_inc(self.hidden, 1)


def add_gated(k, dve, gate, added):
    for j in range(KC):
        dve.scalar_tensor_tensor(k.xT[:, j], half(k.ps, 8 + j), gate[:, j:j + 1], k.xT[:, j], ALU.mult, ALU.add).then_inc(added, 1)


def ffn(k, gate):
    g0 = k.start["ffn"]
    F = FF // 512
    with ExitStack() as ctx:
        tiles = (k.sb("ffn_silu", [P, 4, T], ctx=ctx), k.sb("ffn_hidden", [P, 4, T], ctx=ctx), k.sb("ffn_zero", [P, 512], ctx=ctx))
        with k.stage("ffn") as st:
            block = st.block
            zeroed, out_done, added, *signals = st.signals(7)
            mlp = DenseSwiglu(k, g0, tiles, signals, k.used, k.used, lambda dve, it: dve.wait_ge(k.used, it * R + g0))

            @block.gpsimd
            def _(pool):
                st.clear_last(pool)
                pool.memset(mlp.zero[:], 0.0).then_inc(zeroed, 1)

            @block.sync
            def _(sp):
                k.issue(sp, g0 + R * F + R)

            @block.tensor
            def _(pe):
                pe.wait_ge(zeroed, 1)
                mlp.bound(pe, True)
                with pe.Fori(0, F) as f:
                    mlp.products(pe, f)
                mlp.bound(pe, False).then_inc(out_done, 1)

            @block.scalar
            def _(act):
                with act.Fori(0, F) as f:
                    mlp.silus(act, f)

            @block.vector
            def _(dve):
                dve.sem_inc(mlp.hidden, 1)
                with dve.Fori(0, F) as f:
                    mlp.gates(dve, 0, f)
                dve.wait_ge(out_done, 1)
                add_gated(k, dve, gate, added)


def moe(k, gate, weight, gathered, scatter, largest):
    g0 = k.start["moe"]
    F = FF // 512
    rounds = NE * F
    with ExitStack() as ctx:
        tiles = (k.sb("moe_silu", [P, 4, T], ctx=ctx), k.sb("moe_hidden", [P, 4, T], ctx=ctx), k.sb("moe_zero", [P, 512], ctx=ctx))
        outs = k.sb("expert_out", [P, NE, D], ctx=ctx)
        expert = k.sb("expert_in_turn", [P, KC, P], ctx=ctx)
        turned_hidden = k.sb("hidden_turned", [P, 2, 4, P], ctx=ctx)
        with k.stage("moe") as st:
            block = st.block
            zeroed, out_done, added, up_used, down_used, *dense = st.signals(9)
            silued, hidden, turned, copied, out_moved, tokens_in = st.signals(6)
            mlp = DenseSwiglu(k, g0, tiles, dense, up_used, down_used, lambda dve, it: dve.wait_ge(down_used, it + 2), weight)
            silu = tiles[0][:].rearrange("p (z a) t -> p z (a t)", z=2)
            hid = tiles[1][:].rearrange("p (z a) t -> p z (a t)", z=2)

            @block.gpsimd
            def _(pool):
                st.clear_last(pool)
                pool.memset(mlp.zero[:], 0.0).then_inc(zeroed, 1)
                tokens = pool.value_load(largest[0:1, 0:1], min_val=0, max_val=T)
                with pool.If(tokens <= P):
                    pool.tensor_copy(expert[:], gathered[:, :, 0:P]).then_inc(tokens_in, 1)
                    with pool.Fori(1, NE) as e:
                        pool.wait_ge(up_used, e * (2 * F))
                        pool.tensor_copy(expert[:], gathered[:, :, bass.ds(e * P, P)]).then_inc(tokens_in, 1)

            def over(eng, body):
                with eng.Fori(0, NE) as e:
                    with eng.Fori(0, F) as f:
                        body(e, e * F + f)

            @block.sync
            def _(sp):
                w1 = k.a["moe_w1"][0].rearrange("e (c p) n -> p e c n", p=P)
                w3 = k.a["moe_w3"][0].rearrange("e (c p) n -> p e c n", p=P)
                w2 = k.a["moe_w2"][0].rearrange("e (b p) n -> p (e b) n", p=P)

                def up(e, f):
                    for q, w in enumerate((w1, w3)):
                        sp.wait_ge(up_used, (e * F + f) * 2 + (q - 1))
                        sp.dma_start(k.ring[:, (g0 + q) % R].rearrange("p (c n) -> p c n", c=KC),
                                     w[:, bass.ds(e, 1), :, bass.ds(f * 512, 512)].rearrange("p e c n -> p (e c) n")
                                     ).then_inc(k.loaded[(g0 + q) % R], 16)

                def down(it):
                    sp.wait_ge(down_used, it + 2)
                    sp.dma_start(k.ring[:, (g0 + 2) % R].rearrange("p (b n) -> p b n", b=4),
                                 w2[:, bass.ds(it * 4, 4), :]).then_inc(k.loaded[(g0 + 2) % R], 16)

                up(0, 1)
                with sp.Fori(2, F) as f:
                    up(0, f)
                    down(f - 1)
                with sp.Fori(1, NE) as e:
                    with sp.Fori(0, F) as f:
                        up(e, f)
                        down(e * F + f - 1)
                down(rounds - 1)
                k.issued = g0 + R * rounds
                k.issue(sp, g0 + R * rounds + R)

            @block.tensor
            def _(pe):
                pe.wait_ge(zeroed, 1)
                tokens = pe.value_load(largest[0:1, 0:1], min_val=0, max_val=T)
                with pe.If(tokens > P):
                    mlp.bound(pe, True)
                    over(pe, lambda e, it: mlp.products(pe, it))
                    mlp.bound(pe, False).then_inc(out_done, 1)
                with pe.If(tokens <= P):
                    with pe.Fori(0, NE) as e:
                        def up(f):
                            it = e * F + f
                            if f == 0:
                                pe.wait_ge(tokens_in, e + 1)
                            pe.wait_ge(hidden, it + 1)
                            for q in range(2):
                                pe.wait_ge(k.loaded[(g0 + q) % R], k.load_value(g0 + q, it))
                                w = k.ring[:, (g0 + q) % R].rearrange("p (c n) -> p c n", c=KC)
                                for c in range(KC):
                                    mm = pe.matmul(k.ps[:, 2 * (f % 2) + q, :], expert[:, c], w[:, c],
                                                   start=(c == 0), stop=(c == KC - 1))
                                mm.then_inc(up_used, 1)

                        def turn(f):
                            it = e * F + f
                            pe.wait_ge(hidden, it + 3)
                            pe.wait_ge(copied, it + 1)
                            for j in range(4):
                                mm = pe.transpose(k.ps[:, 4 + f % 2, j * P:(j + 1) * P], hid[:, f % 2, j * P:(j + 1) * P], k.ident)
                            mm.then_inc(turned, 1)

                        def down(f):
                            it = e * F + f
                            pe.wait_ge(copied, it + 3)
                            pe.wait_ge(k.loaded[(g0 + 2) % R], k.load_value(g0 + 2, it))
                            if f == 0:
                                pe.wait_ge(out_moved, e + 1)
                            w2 = k.ring[:, (g0 + 2) % R].rearrange("p (b n) -> p b n", b=4)
                            for j in range(4):
                                for d in range(2):
                                    mm = pe.matmul(k.ps[:, 6 + d, :], turned_hidden[:, f % 2, j], w2[:, j, d * 512:(d + 1) * 512],
                                                   start=(f == 0 and j == 0), stop=(f == F - 1 and j == 3))
                            mm.then_inc(down_used, 1)

                        for f in range(F):
                            up(f)
                            if f > 0:
                                down(f - 1)
                            turn(f)
                        down(F - 1)
                    pe.wait_ge(out_moved, NE + 1)
                    for d in range(KC):
                        for e in range(NE):
                            mm = pe.matmul(half(k.ps, 8 + d), outs[:, e, d * P:(d + 1) * P], scatter[:, e],
                                           start=(e == 0), stop=(e == NE - 1))
                    mm.then_inc(out_done, 1)

            @block.scalar
            def _(act):
                tokens = act.value_load(largest[0:1, 0:1], min_val=0, max_val=T)
                with act.If(tokens > P):
                    over(act, lambda e, it: mlp.silus(act, it))
                with act.If(tokens <= P):
                    act.sem_inc(copied, 2)
                    act.sem_inc(out_moved, 1)
                    with act.Fori(0, NE) as e:
                        for f in range(F):
                            it = e * F + f
                            act.wait_ge(up_used, it * 2 + 1)
                            act.wait_ge(hidden, it + 1)
                            act.activation(silu[:, f % 2], k.ps[:, 2 * (f % 2), :], ACT.Silu).then_inc(silued, 1)
                            act.wait_ge(turned, it + 3)
                            act.wait_ge(down_used, it + 1)
                            act.activation(turned_hidden[:, f % 2], k.ps[:, 4 + f % 2, :].rearrange("p (j t) -> p j t", j=4),
                                           ACT.Copy).then_inc(copied, 1)
                        act.wait_ge(down_used, e * F + (F + 2))
                        act.activation(outs[:, bass.ds(e, 1)], k.ps[:, 6:8, :].rearrange("p b n -> p (b n)").unsqueeze(1),
                                       ACT.Copy).then_inc(out_moved, 1)
                act.wait_ge(out_done, 1)
                act.sem_inc(k.used, R * rounds)

            @block.vector
            def _(dve):
                tokens = dve.value_load(largest[0:1, 0:1], min_val=0, max_val=T)
                dve.sem_inc(down_used, 2)
                with dve.If(tokens > P):
                    dve.sem_inc(mlp.hidden, 1)
                    over(dve, lambda e, it: mlp.gates(dve, e, it))
                with dve.If(tokens <= P):
                    dve.sem_inc(hidden, 2)
                    dve.sem_inc(turned, 2)
                    with dve.Fori(0, NE) as e:
                        for f in range(F):
                            it = e * F + f
                            dve.wait_ge(silued, it + 1)
                            dve.wait_ge(up_used, it * 2 + 2)
                            dve.wait_ge(turned, it + 1)
                            dve.tensor_tensor(hid[:, f % 2], silu[:, f % 2], k.ps[:, 2 * (f % 2) + 1, :], ALU.mult).then_inc(hidden, 1)
                dve.wait_ge(out_done, 1)
                add_gated(k, dve, gate, added)


def router(k, weight, gathered, scatter, largest):
    with ExitStack() as ctx:
        lg = k.sb("logits", [P, TT, NE], ctx=ctx)
        top = k.sb("logits_top", [P, TT, 8], ctx=ctx)
        ix = k.sb("logits_ix", [P, TT, 8], U32, ctx=ctx)
        ixf = k.sb("logits_ixf", [P, TT, 8], ctx=ctx)
        pr = k.sb("top_p", [P, TT, 2], ctx=ctx)
        wt = k.sb("token_weights", [P, TT, NE], ctx=ctx)
        w2 = k.sb("token_weights2", [P, TT, NE], ctx=ctx)
        chosen = k.sb("token_chosen", [P, TT, NE], ctx=ctx)
        rank = k.sb("token_rank", [P, TT, NE], ctx=ctx)
        count = k.sb("expert_count", [P, 8], ctx=ctx)
        select = k.sb("token_select", [P, TT, NE, P], ctx=ctx)
        select_w = k.sb("token_select_weight", [P, TT, NE, P], ctx=ctx)
        h_rows = k.sb("h_rows", [P, TT, D], ctx=ctx)
        wr = k.sb("weights_turned", [NE, T], ctx=ctx)
        with k.stage("router") as st:
            block = st.block
            scored, chain, apart, exped, weighed, turned, turned_out, spread, moved = st.signals(9)

            @block.gpsimd
            def _(pool):
                st.clear_last(pool)

            @block.tensor
            def _(pe):
                for i in range(TT):
                    o = k.ps[:, i, 0:NE]
                    for c in range(KC):
                        pe.matmul(o, k.h[:, c, i * P:(i + 1) * P], k.wrt[:, c, :], start=(c == 0), stop=False)
                    mm = pe.matmul(o, k.ones[0:1, :], k.rb[:], start=False, stop=True)
                mm.then_inc(scored, 1)
                pe.wait_ge(weighed, 1)
                for i in range(TT):
                    mm = pe.transpose(k.ps[0:NE, 2, i * P:(i + 1) * P], wt[:, i, :], k.ident)
                mm.then_inc(turned, 1)
                pe.wait_ge(turned_out, 1)
                for e in range(NE):
                    mm = pe.matmul(half(k.ps, 8 + e), k.ident[0:NE, e:e + 1].to_broadcast([NE, P]), wr[:], start=True, stop=True)
                mm.then_inc(spread, 1)

            @block.vector
            def _(dve):
                link = Chain(dve, chain)
                dve.wait_ge(scored, 1)
                link(dve.tensor_copy(lg[:], k.ps[:, 0:2, 0:NE]))
                for i in range(TT):
                    link(dve.max(top[:, i], lg[:, i]))
                    link(dve.max_index(ix[:, i], top[:, i], lg[:, i]))
                link(dve.tensor_copy(ixf[:], ix[:]))
                dve.tensor_tensor(pr[:, :, 1], top[:, :, 1], top[:, :, 0], ALU.subtract).then_inc(apart, 1)
                dve.wait_ge(exped, 1)
                link(dve.tensor_scalar(pr[:, :, 0], pr[:, :, 1], 1.0, None, ALU.add))
                link(dve.reciprocal(pr[:, :, 0], pr[:, :, 0]))
                link(dve.tensor_tensor(pr[:, :, 1], pr[:, :, 1], pr[:, :, 0], ALU.mult))
                for i in range(TT):
                    link(dve.tensor_scalar(wt[:, i], k.iota[:, 0:NE], ixf[:, i, 0:1], pr[:, i, 0:1], ALU.is_equal, ALU.mult))
                    link(dve.tensor_scalar(w2[:, i], k.iota[:, 0:NE], ixf[:, i, 1:2], pr[:, i, 1:2], ALU.is_equal, ALU.mult))
                dve.tensor_tensor(wt[:], wt[:], w2[:], ALU.add).then_inc(weighed, 1)
                for i in range(TT):
                    link(dve.tensor_scalar(chosen[:, i], k.iota[:, 0:NE], ixf[:, i, 0:1], None, ALU.is_equal))
                    link(dve.tensor_scalar(w2[:, i], k.iota[:, 0:NE], ixf[:, i, 1:2], None, ALU.is_equal))
                link(dve.tensor_tensor(chosen[:], chosen[:], w2[:], ALU.add))

            @block.scalar
            def _(act):
                act.wait_ge(apart, 1)
                act.activation(pr[:, :, 1], pr[:, :, 1], ACT.Exp).then_inc(exped, 1)
                act.wait_ge(turned, 1)
                act.activation(wr[:], k.ps[0:NE, 2, 0:T], ACT.Copy).then_inc(turned_out, 1)
                act.wait_ge(spread, 1)
                act.activation(weight[:], place_rows(k.ps, P)[:, 8:16], ACT.Copy).then_inc(moved, 1)

        with k.stage("dispatch") as st:
            block = st.block
            ranked, chain, selected, rows_turned, rows_moved, weights_turned, bank_free, filled, moved = st.signals(9)

            @block.gpsimd
            def _(pool):
                st.clear_last(pool)

            @block.tensor
            def _(pe):
                pe.matmul(k.ps[:, 0, 0:NE], k.msk_lt, chosen[:, 0], start=True, stop=True)
                pe.matmul(k.ps[:, 0, NE:2 * NE], k.ones, chosen[:, 0], start=True, stop=False)
                pe.matmul(k.ps[:, 0, NE:2 * NE], k.msk_lt, chosen[:, 1], start=False, stop=True)
                pe.matmul(k.ps[:, 0, 2 * NE:3 * NE], k.ones, chosen[:, 0], start=True, stop=False)
                pe.matmul(k.ps[:, 0, 2 * NE:3 * NE], k.ones, chosen[:, 1], start=False, stop=True).then_inc(ranked, 1)
                for i in range(TT):
                    for c in range(KC):
                        mm = pe.transpose(k.ps[:, 1 + 2 * i + c // 4, (c % 4) * P:(c % 4 + 1) * P], k.h[:, c, i * P:(i + 1) * P], k.ident)
                mm.then_inc(rows_turned, 1)
                pe.wait_ge(selected, 2)
                pe.wait_ge(rows_moved, 1)
                for e in range(NE):
                    for i in range(TT):
                        mm = pe.transpose(half(k.ps, 2 + e)[:, i * P:(i + 1) * P], select_w[:, i, e], k.ident)
                mm.then_inc(weights_turned, 1)
                for c in range(KC):
                    b = 6 if c % 2 == 0 else 2
                    if c == 1:
                        pe.wait_ge(bank_free, 1)
                    if c > 1:
                        pe.wait_ge(moved, c - 1)
                    for half_e in range(2):
                        for i in range(TT):
                            mm = pe.matmul(k.ps[:, b + half_e, :], h_rows[:, i, c * P:(c + 1) * P],
                                           select[:, i, 4 * half_e:4 * half_e + 4].rearrange("p e s -> p (e s)"),
                                           start=(i == 0), stop=(i == TT - 1))
                    mm.then_inc(filled, 1)

            @block.vector
            def _(dve):
                link = Chain(dve, chain)
                dve.wait_ge(ranked, 1)
                link(dve.tensor_copy(rank[:].rearrange("p i e -> p (i e)"), k.ps[:, 0, 0:2 * NE]))
                link(dve.max(count[:], k.ps[:, 0, 2 * NE:3 * NE]))
                link(dve.tensor_copy(largest[:], count[0:1, 0:1]))
                for out, by in ((select_w, wt), (select, chosen)):
                    for e in range(NE):
                        for i in range(TT):
                            ins = dve.tensor_scalar(out[:, i, e], k.iota, rank[:, i, e:e + 1], by[:, i, e:e + 1], ALU.is_equal, ALU.mult)
                    ins.then_inc(selected, 1)

            @block.scalar
            def _(act):
                act.wait_ge(rows_turned, 1)
                act.activation(h_rows[:].rearrange("p i d -> p (i d)"), k.ps[:, 1:5, :].rearrange("p b n -> p (b n)"),
                               ACT.Copy).then_inc(rows_moved, 1)
                act.wait_ge(weights_turned, 1)
                act.activation(scatter[:], place_rows(k.ps, P)[:, 2:10], ACT.Copy).then_inc(bank_free, 1)
                for c in range(KC):
                    b = 6 if c % 2 == 0 else 2
                    act.wait_ge(filled, c + 1)
                    act.activation(gathered[:, c], k.ps[:, b:b + 2, :].rearrange("p b n -> p (b n)"), ACT.Copy).then_inc(moved, 1)


def memory_keys(k, mk, mv):
    with ExitStack() as ctx:
        mt = k.sb("memT", [P, KC, T], ctx=ctx)
        with ExitStack() as c2:
            rows = k.sb("mem_rows", [P, TT, D], ctx=c2)
            with k.stage("memory_load") as st:
                block = st.block
                in_mem, turned, moved = st.signals(3)

                @block.gpsimd
                def _(pool):
                    st.clear_last(pool)

                @block.sync
                def _(sp):
                    sp.dma_start(rows[:], k.a["mem_2"][0].rearrange("(i p) d -> p i d", p=P)).then_inc(in_mem, 16)

                @block.tensor
                def _(pe):
                    pe.wait_ge(in_mem, 16)
                    for c in range(KC):
                        for i in range(TT):
                            mm = pe.transpose(half(k.ps, c)[:, i * P:(i + 1) * P], rows[:, i, c * P:(c + 1) * P], k.ident)
                    mm.then_inc(turned, 1)

                @block.scalar
                def _(act):
                    act.wait_ge(turned, 1)
                    act.activation(mt[:], place_rows(k.ps, P)[:, 0:KC], ACT.Copy).then_inc(moved, 1)
        rms(k, "memory_norm", mt, mt, k.col("mem_norm_2", 0, 8))
        k.proj = k.sb("mem_proj", [P, 12, T], ctx=ctx)
        linear(k, "mem_kv", 3, mt, k.proj, 0)
        masks = k.sb("mem_heads", [P, 9, P], ctx=ctx)
        load_table(k, "table_memh", masks[:].rearrange("p n t -> p (n t)"))
        memory_unit(k, "memory_k_norm", 0, "mem_k", masks)
        with k.stage("memory_k_move") as st:
            moved, = st.signals(1)

            @st.block.gpsimd
            def _(pool):
                st.clear_last(pool)

            @st.block.scalar
            def _(act):
                act.activation(mk[:], k.proj[:, 0:6], ACT.Copy).then_inc(moved, 1)
        to_tokens(k, "memory_turn", 6, 6, mv)


def load_table(k, name, dst):
    with k.stage(name) as st:
        in_table, = st.signals(1)

        @st.block.gpsimd
        def _(pool):
            st.clear_last(pool)

        @st.block.sync
        def _(sp):
            sp.dma_start(dst, k.a[name]).then_inc(in_table, 16)
            sp.wait_ge(in_table, 16)


def memory_unit(k, name, b0, w, masks):
    with ExitStack() as ctx:
        sq = k.sb(f"sq_{name}", [P, 6, T], ctx=ctx)
        with k.stage(name) as st:
            block = st.block
            squared, summed, mean, root, chain = st.signals(5)

            @block.gpsimd
            def _(pool):
                st.clear_last(pool)

            @block.scalar
            def _(act):
                act.activation(sq[:], k.proj[:, b0:b0 + 6], ACT.Square).then_inc(squared, 1)
                act.wait_ge(mean, 1)
                act.activation(sq[:], sq[:], ACT.Sqrt).then_inc(root, 1)

            @block.tensor
            def _(pe):
                pe.wait_ge(squared, 1)
                for b in range(6):
                    src = [c for c in range(3) if (c, b % 3) not in ((0, 2), (2, 0))]
                    for n, c in enumerate(src):
                        mm = pe.matmul(half(k.ps, b), masks[:, 3 * c + b % 3], sq[:, b // 3 * 3 + c],
                                       start=(n == 0), stop=(n == len(src) - 1))
                mm.then_inc(summed, 1)

            @block.vector
            def _(dve):
                link = Chain(dve, chain)
                dve.wait_ge(summed, 1)
                dve.tensor_scalar(sq[:], place_rows(k.ps, P)[:, 0:6], 1.0 / MD, EPS, ALU.mult, ALU.add).then_inc(mean, 1)
                dve.wait_ge(root, 1)
                link(dve.reciprocal(sq[:], sq[:]))
                for b in range(6):
                    x = k.proj[:, b0 + b]
                    link(dve.scalar_tensor_tensor(x, x, k.col(w, b % 3, 1), sq[:, b], ALU.mult, ALU.mult))


def ssd(k):
    W = T + P
    with ExitStack() as ctx:
        acol = k.sb("ssd_acol", [P, TT, SSH], ctx=ctx)
        dtcol = k.sb("ssd_dtcol", [P, TT, SSH], ctx=ctx)
        g = k.sb("ssd_sums", [SSH, T], ctx=ctx)
        head_gates(k, "ssd_gates", k.wdt, SSH, 4, acol, None, whole=True, out_b=dtcol, keep=g)
        conv_silu(k, "ssd_conv", XS0, 16, "conv_2", "conv_b_2")
        xdt = k.sb("ssd_xdt", [P, TT, D], ctx=ctx)
        cb = k.sb("ssd_cb", [P, SSG, W], ctx=ctx)
        with k.stage("ssd_products") as st:
            block = st.block
            turned, multiplied, moved = st.signals(3)

            @block.gpsimd
            def _(pool):
                st.clear_last(pool)

            @block.tensor
            def _(pe):
                for b in range(8):
                    for i in range(TT):
                        mm = pe.transpose(half(k.ps, b)[:, i * P:(i + 1) * P], k.proj[:, XS0 + b, i * P:(i + 1) * P], k.ident)
                mm.then_inc(turned, 1)
                for q in range(SSG):
                    pe.matmul(k.ps[:, 4 + q, 0:T], k.proj[:, BM0 + q, 0:P], k.proj[:, CM0 + q, :], start=True, stop=True)
                    mm = pe.matmul(k.ps[:, 4 + q, T:W], k.proj[:, BM0 + q, P:T], k.proj[:, CM0 + q, P:T], start=True, stop=True)
                mm.then_inc(multiplied, 1)

            @block.vector
            def _(dve):
                dve.wait_ge(turned, 1)
                for i in range(TT):
                    src = place_rows(k.ps, P)[:, 0:8, i * P:(i + 1) * P].rearrange("p b (h e) -> p b h e", h=2)
                    dt = dtcol[:, i].rearrange("p (b h) -> p b h", b=8).unsqueeze(3).to_broadcast([P, 8, 2, 64])
                    dve.tensor_tensor(xdt[:, i].rearrange("p (b h e) -> p b h e", b=8, h=2), src, dt, ALU.mult).then_inc(moved, 1)

            @block.scalar
            def _(act):
                act.wait_ge(multiplied, 1)
                act.activation(cb[:], k.ps[:, 4:8, 0:W], ACT.Copy).then_inc(moved, 1)
        dec = k.sb("ssd_decay", [P, 4, W], ctx=ctx)
        with k.stage("ssd_heads") as st:
            block = st.block
            spread, placed, exped, chain, weights, out_ready, out_taken = st.signals(7)
            H = SSH

            @block.gpsimd
            def _(pool):
                st.clear_last(pool)

            @block.tensor
            def _(pe):
                def row(h):
                    if h >= 2:
                        pe.wait_ge(placed, 3 * (h - 1))
                    pe.matmul(k.ps[:, h % 2, 0:T], k.ident[0:SSH, h:h + 1].to_broadcast([SSH, P]), g[:], start=True, stop=True).then_inc(spread, 1)

                def mix(h):
                    pe.wait_ge(weights, h + 1)
                    if h >= 4 and h % 2 == 0:
                        pe.wait_ge(out_taken, h // 2 - 1)
                    r0 = 64 * (h % 2)
                    o = k.ps[r0:r0 + 64, 4 + (h // 2) % 2, :]
                    pe.matmul(o[:, 0:T], xdt[:, 0, 64 * h:64 * h + 64], dec[:, h % 4, 0:T], start=True, stop=False, skip_group_check=True)
                    pe.matmul(o[:, P:T], xdt[:, 1, 64 * h:64 * h + 64], dec[:, h % 4, T:W], start=False, stop=True, skip_group_check=True).then_inc(out_ready, 1)
                for i in range(H + 2):
                    if i < H:
                        row(i)
                    if i >= 2:
                        mix(i - 2)

            @block.vector
            def _(dve):
                def place(h):
                    dve.wait_ge(spread, h + 1)
                    if h >= 4:
                        dve.wait_ge(out_ready, h - 3)
                    d, r = dec[:, h % 4], k.ps[:, h % 2, :]
                    a0, a1 = acol[:, 0, h:h + 1], acol[:, 1, h:h + 1]
                    dve.scalar_tensor_tensor(d[:, 0:P], r[:, 0:P], a0, k.neg_le, ALU.subtract, ALU.add).then_inc(placed, 1)
                    dve.tensor_scalar(d[:, P:T], r[:, P:T], a0, None, ALU.subtract).then_inc(placed, 1)
                    dve.scalar_tensor_tensor(d[:, T:W], r[:, P:T], a1, k.neg_le, ALU.subtract, ALU.add).then_inc(placed, 1)

                def times(h):
                    dve.wait_ge(exped, h + 1)
                    dve.tensor_tensor(dec[:, h % 4], dec[:, h % 4], cb[:, h // 4], ALU.mult).then_inc(weights, 1)

                def take(b):
                    dve.wait_ge(out_ready, 2 * b + 2)
                    dve.scalar_tensor_tensor(k.o[:, b], k.proj[:, XS0 + b], k.col("ssd_d", b, 1), k.ps[:, 4 + b % 2, 0:T],
                                             ALU.mult, ALU.add).then_inc(out_taken, 1)
                for i in range(H + 3):
                    if i < H:
                        place(i)
                    if 0 <= i - 1 < H:
                        times(i - 1)
                    if i >= 3 and (i - 3) % 2 == 1:
                        take((i - 3) // 2)

            @block.scalar
            def _(act):
                for h in range(H):
                    act.wait_ge(placed, 3 * h + 3)
                    act.activation(dec[:, h % 4], dec[:, h % 4], ACT.Exp).then_inc(exped, 1)
    with ExitStack() as ctx:
        sq = k.sb("ssd_sq", [P, 8, T], ctx=ctx)
        rs = k.sb("ssd_rs", [P, 4, T], ctx=ctx)
        with k.stage("ssd_norm") as st:
            block = st.block
            gated, squared, summed, mean, root, chain = st.signals(6)
            z = k.proj[:, ZZ0:ZZ0 + 8]

            @block.gpsimd
            def _(pool):
                st.clear_last(pool)

            @block.scalar
            def _(act):
                act.activation(z, z, ACT.Silu).then_inc(squared, 1)
                act.wait_ge(gated, 1)
                act.activation(sq[:], k.o[:, 0:8], ACT.Square).then_inc(squared, 1)
                act.wait_ge(mean, 1)
                act.activation(rs[:], rs[:], ACT.Sqrt).then_inc(root, 1)

            @block.tensor
            def _(pe):
                pe.wait_ge(squared, 2)
                for q in range(SSG):
                    for e in range(2):
                        mm = pe.matmul(half(k.ps, q), k.ones, sq[:, 2 * q + e], start=(e == 0), stop=(e == 1))
                mm.then_inc(summed, 1)

            @block.vector
            def _(dve):
                link = Chain(dve, chain)
                dve.wait_ge(squared, 1)
                o = k.o[:, 0:8]
                dve.tensor_tensor(o, o, z, ALU.mult).then_inc(gated, 1)
                dve.wait_ge(summed, 1)
                dve.tensor_scalar(rs[:], place_rows(k.ps, P)[:, 0:4], 1.0 / (2 * P), EPS, ALU.mult, ALU.add).then_inc(mean, 1)
                dve.wait_ge(root, 1)
                link(dve.reciprocal(rs[:], rs[:]))
                dve.wait_ge(gated, 1)
                for b in range(8):
                    link(dve.scalar_tensor_tensor(k.o[:, b], k.o[:, b], k.col("ssd_norm_2", b, 1), rs[:, b // 2], ALU.mult, ALU.mult))


TWO_PI = 2 * np.pi
PI_1 = 6.28125
PI_2 = float(np.round((TWO_PI - PI_1) * 2 ** 20) / 2 ** 20)
PI_3 = float(np.float32(TWO_PI - PI_1 - PI_2))
ROUND = 12582912.0
PI_MAX = 3.1415925


def rope(k):
    with ExitStack() as ctx:
        posi = k.sb("positions", [1, T], I32, ctx=ctx)
        posf = k.sb("positions_f", [1, T], ctx=ctx)
        ang = k.sb("angle", [P, T], ctx=ctx)
        turn = k.sb("turns", [P, T], ctx=ctx)
        sn = k.sb("sin", [P, T], ctx=ctx)
        cs = k.sb("cos", [P, T], ctx=ctx)
        tmp = k.sb("rope_tmp", [P, 6, T], ctx=ctx)
        with k.stage("rope") as st:
            block = st.block
            in_pos, pos_f, spread, chain, angled, sined, rotated, done = st.signals(8)

            @block.gpsimd
            def _(pool):
                st.clear_last(pool)

            @block.sync
            def _(sp):
                sp.dma_start(posi[:], k.a["positions_2"]).then_inc(in_pos, 16)

            @block.tensor
            def _(pe):
                for c in range(6):
                    pe.matmul(k.ps[:, c, :], k.perm, k.proj[:, DQ0 + 2 * c:DQ0 + 2 * c + 2], start=True, stop=True).then_inc(rotated, 1)
                pe.wait_ge(pos_f, 1)
                pe.matmul(k.ps[:, 7, 0:T], k.ones[0:1, :], posf[:], start=True, stop=True).then_inc(spread, 1)

            @block.vector
            def _(dve):
                link = Chain(dve, chain)
                dve.wait_ge(in_pos, 16)
                dve.tensor_copy(posf[:], posi[:]).then_inc(pos_f, 1)
                dve.wait_ge(spread, 1)
                link(dve.tensor_scalar(ang[:], k.ps[:, 7, 0:T], k.inv, None, ALU.mult))
                link(dve.tensor_scalar(turn[:], ang[:], 1.0 / TWO_PI, None, ALU.mult))
                link(dve.tensor_scalar(turn[:], turn[:], ROUND, None, ALU.add))
                link(dve.tensor_scalar(turn[:], turn[:], ROUND, None, ALU.subtract))
                for c in (PI_1, PI_2, PI_3):
                    link(dve.scalar_tensor_tensor(ang[:], turn[:], -c, ang[:], ALU.mult, ALU.add))
                link(dve.tensor_scalar(sn[:], ang[:], PI_MAX, -PI_MAX, ALU.min, ALU.max))
                link(dve.tensor_scalar(cs[:], ang[:], float(np.pi / 2), None, ALU.add))
                link(dve.tensor_scalar(turn[:], cs[:], float(np.pi), TWO_PI, ALU.is_gt, ALU.mult))
                link(dve.tensor_tensor(cs[:], cs[:], turn[:], ALU.subtract))
                dve.tensor_scalar(cs[:], cs[:], PI_MAX, -PI_MAX, ALU.min, ALU.max).then_inc(angled, 1)
                dve.wait_ge(sined, 2)
                dve.wait_ge(rotated, 6)
                for m in range(2):
                    x = k.proj[:, DQ0 + 6 * m:DQ0 + 6 * m + 6]
                    link(dve.tensor_tensor(tmp[:], place_rows(k.ps, P)[:, 6 * m:6 * m + 6], row_bc(sn[:], 6), ALU.mult))
                    link(dve.tensor_tensor(x, x, row_bc(cs[:], 6), ALU.mult))
                    link(dve.tensor_tensor(x, x, tmp[:], ALU.add))

            @block.scalar
            def _(act):
                act.wait_ge(angled, 1)
                act.activation(sn[:], sn[:], ACT.Sin).then_inc(sined, 1)
                act.activation(cs[:], cs[:], ACT.Sin).then_inc(sined, 1)


def softmax_heads(k, name, n_items, width, score, scale, mask, mix, n_out, dst0):
    WM = max(width(n) for n in range(n_items))
    with ExitStack() as ctx:
        sc = k.sb(f"scores_{name}", [P, 2, WM], ctx=ctx)
        pt = k.sb(f"probs_{name}", [P, WM], ctx=ctx)
        st_ = k.sb(f"stats_{name}", [P, 4, 2], ctx=ctx)
        with k.stage(name) as st:
            block = st.block
            scored, maxed, exped, chain, normed, turned, moved, mixed = st.signals(8)

            def flat(b):
                return k.ps[:, b:b + 2, :].rearrange("p b t -> p (b t)")

            @block.gpsimd
            def _(pool):
                st.clear_last(pool)

            @block.tensor
            def _(pe):
                def first(n):
                    if n >= 2:
                        pe.wait_ge(maxed, n - 1)
                    score(pe, n, flat(2 * (n % 2))).then_inc(scored, 1)

                def turn(n):
                    pe.wait_ge(normed, n + 1)
                    if n:
                        pe.wait_ge(moved, n)
                    for b in range(width(n) // P):
                        mm = pe.transpose(flat(4)[:, b * P:(b + 1) * P], sc[:, n % 2, b * P:(b + 1) * P], k.ident)
                    mm.then_inc(turned, 1)

                def last(n):
                    pe.wait_ge(moved, n + 1)
                    mix(pe, n, pt).then_inc(mixed, 1)
                for i in range(n_items + 2):
                    if i < n_items:
                        first(i)
                    if i >= 2:
                        last(i - 2)
                    if 1 <= i <= n_items:
                        turn(i - 1)

            @block.vector
            def _(dve):
                link = Chain(dve, chain)

                def first(n):
                    dve.wait_ge(scored, n + 1)
                    if n >= 2:
                        dve.wait_ge(turned, n - 1)
                    w, s = width(n), sc[:, n % 2]
                    if mask is None:
                        link(dve.tensor_scalar(s[:, 0:w], flat(2 * (n % 2))[:, 0:w], scale, None, ALU.mult))
                    else:
                        link(dve.scalar_tensor_tensor(s[:, 0:w], flat(2 * (n % 2))[:, 0:w], scale, mask(n), ALU.mult, ALU.add))
                    link(dve.tensor_reduce(st_[:, 0, n % 2:n % 2 + 1], s[:, 0:w], AX.X, ALU.max))
                    dve.tensor_scalar(st_[:, 1, n % 2:n % 2 + 1], st_[:, 0, n % 2:n % 2 + 1], -1.0, None, ALU.mult).then_inc(maxed, 1)

                def second(n):
                    dve.wait_ge(exped, n + 1)
                    r = st_[:, 3, n % 2:n % 2 + 1]
                    link(dve.reciprocal(r, st_[:, 2, n % 2:n % 2 + 1]))
                    s = sc[:, n % 2, 0:width(n)]
                    dve.tensor_scalar(s, s, r, None, ALU.mult).then_inc(normed, 1)
                for i in range(n_items + 1):
                    if i < n_items:
                        first(i)
                    if i >= 1:
                        second(i - 1)

            @block.scalar
            def _(act):
                def prob(n):
                    act.wait_ge(maxed, n + 1)
                    s = sc[:, n % 2, 0:width(n)]
                    act.activation(s, s, ACT.Exp, bias=st_[:, 1, n % 2:n % 2 + 1], accum_out=st_[:, 2, n % 2:n % 2 + 1]).then_inc(exped, 1)

                def move(n):
                    act.wait_ge(turned, n + 1)
                    if n:
                        act.wait_ge(mixed, n)
                    act.activation(pt[:, 0:width(n)], flat(4)[:, 0:width(n)], ACT.Copy).then_inc(moved, 1)
                for i in range(n_items + 1):
                    if i < n_items:
                        prob(i)
                    if i >= 1:
                        move(i - 1)
                act.wait_ge(mixed, n_items)
                for j in range(n_out):
                    act.activation(k.o[:, dst0 + j], half(k.ps, 12 + j), ACT.Copy).then_inc(moved, 1)


def dilated(k):
    rope_heads = [(DQ0, 6, 1.0 / 64, EPS, k.col("dil_q", 0, 1)), (DK0, 6, 1.0 / 64, EPS, k.col("dil_k", 0, 1))]
    unit_rows(k, "dilated_norm", rope_heads, k.ones64)
    rope(k)
    with ExitStack() as ctx:
        vt = k.sb("dil_v", [P, TT, 6 * P], ctx=ctx)
        masks = k.sb("dil_masks", [P, 3 * P + 3 * T], ctx=ctx)
        to_tokens(k, "dilated_turn", DV0, 6, vt)
        load_table(k, "table_dil", masks[:])

        def width(n):
            return 3 * P * (n % 2 + 1)

        def score(pe, n, ps):
            j, i = n // 2, n % 2
            w = P * (i + 1)
            rows = slice(64 * (j % 2), 64 * (j % 2) + 64)
            for g in range(3):
                b = (4 * g + j) // 2
                mm = pe.matmul(ps[:, g * w:(g + 1) * w], k.proj[rows, DQ0 + b, i * P:(i + 1) * P], k.proj[rows, DK0 + b, 0:w],
                               start=True, stop=True)
            return mm

        def mix(pe, n, pt):
            j, i = n // 2, n % 2
            r0 = 64 * (j % 2)
            out = half(k.ps, 12 + j // 2)[r0:r0 + 64, i * P:(i + 1) * P]
            for g in range(3):
                for kt in range(i + 1):
                    b = g * (i + 1) + kt
                    c0 = 64 * (4 * g + j)
                    mm = pe.matmul(out, vt[:, kt, c0:c0 + 64], pt[:, b * P:(b + 1) * P], start=(b == 0), stop=(b == 3 * (i + 1) - 1),
                                   skip_group_check=True)
            return mm
        softmax_heads(k, "dilated_heads", 8, width, score, 64 ** -0.5,
                      lambda n: masks[:, 0:3 * P] if n % 2 == 0 else masks[:, 3 * P:3 * P + 3 * T], mix, 2, 8)


def memory_attention(k, mk, mv):
    with ExitStack() as ctx:
        masks = k.sb("mem_heads2", [P, 9, P], ctx=ctx)
        load_table(k, "table_memh", masks[:].rearrange("p n t -> p (n t)"))
        memory_unit(k, "memory_q_norm", MQ0, "mem_q", masks)
    for pair in range(2):

        def pieces(h):
            b = 3 * pair
            return ((b, 0, 128, 0), (b + 1, 0, 64, 128)) if h == 0 else ((b + 1, 64, 64, 0), (b + 2, 0, 128, 64))

        def score(pe, n, ps):
            h, i = n // 2, n % 2
            for m, (b, r0, nr, _) in enumerate(pieces(h)):
                mm = pe.matmul(ps[:, 0:T], k.proj[r0:r0 + nr, MQ0 + b, i * P:(i + 1) * P], mk[r0:r0 + nr, b, :],
                               start=(m == 0), stop=(m == 1))
            return mm

        def mix(pe, n, pt):
            h, i = n // 2, n % 2
            for b, r0, nr, c0 in pieces(h):
                out = half(k.ps, 12 + b - 3 * pair)[r0:r0 + nr, i * P:(i + 1) * P]
                c = MD * (2 * pair + h) + c0
                for kt in range(2):
                    mm = pe.matmul(out, mv[:, kt, c:c + nr], pt[:, kt * P:(kt + 1) * P], start=(kt == 0), stop=(kt == 1),
                                   skip_group_check=True)
            return mm
        softmax_heads(k, f"memory_heads{pair}", 4, lambda n: T, score, MD ** -0.5, None, mix, 3, 10 + 3 * pair)


def peer_choice(k, i1t, i2t, gt):
    H = PH
    with ExitStack() as ctx:
        qt = k.sb("peer_q", [P, 2 * H, T], ctx=ctx)
        linear(k, "peer_query", 4, k.h, qt, 0, ahead=2)
        sc = k.sb("peer_scores", [P, TT, 2 * H, NK], ctx=ctx)
        with ExitStack() as c2:
            kn = k.sb("peer_keys", [P, 2 * H, P], ctx=c2)
            kt = k.sb("peer_keysT", [P, 2 * H, NK], ctx=c2)
            with k.stage("peer_scores") as st:
                block = st.block
                in_keys, turned, moved, scored, scores_out = st.signals(5)

                @block.gpsimd
                def _(pool):
                    st.clear_last(pool)

                @block.sync
                def _(sp):
                    sp.dma_start(kn[:], k.a["peer_sub_keys_2"][0].rearrange("h c k d -> k (h c) d")).then_inc(in_keys, 16)

                def four(b):
                    return k.ps[:, b:b + 4, :].rearrange("p b (e t) -> p (b e) t", e=4)

                @block.tensor
                def _(pe):
                    pe.wait_ge(in_keys, 16)
                    for n in range(2 * H):
                        mm = pe.transpose(four(0)[:, n], kn[:, n], k.ident)
                    mm.then_inc(turned, 1)
                    pe.wait_ge(moved, 1)
                    for i in range(TT):
                        for n in range(2 * H):
                            mm = pe.matmul(four(4 * (1 - i))[:, n], qt[:, n, i * P:(i + 1) * P], kt[:, n], start=True, stop=True)
                        mm.then_inc(scored, 1)

                @block.scalar
                def _(act):
                    act.wait_ge(turned, 1)
                    act.activation(kt[:], four(0), ACT.Copy).then_inc(moved, 1)
                    for i in range(TT):
                        act.wait_ge(scored, i + 1)
                        act.activation(sc[:, i], four(4 * (1 - i)), ACT.Copy).then_inc(scores_out, 1)
        v = k.sb("peer_best", [P, TT, 2 * H, TOPK], ctx=ctx)
        ix = k.sb("peer_best_ix", [P, TT, 2 * H, TOPK], U32, ctx=ctx)
        ixf = k.sb("peer_best_ixf", [P, TT, 2 * H, TOPK], ctx=ctx)
        top = k.sb("peer_top", [P, TT, H, TOPK], ctx=ctx)
        pos = k.sb("peer_pos", [P, TT, H, TOPK], U32, ctx=ctx)
        pa = k.sb("peer_pos_a", [P, TT, H, TOPK], U32, ctx=ctx)
        pf = k.sb("peer_pos_f", [P, 2, TT, H, TOPK], ctx=ctx)
        key = k.sb("peer_key", [P, 2, TT, H, TOPK], ctx=ctx)
        stat = k.sb("peer_stat", [P, TT, H], ctx=ctx)
        cand = k.sb("peer_cand", [P, 2, TOPK, TOPK], ctx=ctx)
        hot = k.sb("peer_hot", [P, H, TOPK, TOPK], ctx=ctx)
        with k.stage("peer_top") as st:
            block = st.block
            chain, apart, exped, chosen, turned, moved = st.signals(6)

            @block.gpsimd
            def _(pool):
                st.clear_last(pool)

            @block.vector
            def _(dve):
                link = Chain(dve, chain)

                def top16(src, vals, idx):
                    link(dve.max(vals[:, 0:8], src))
                    link(dve.max_index(idx[:, 0:8], vals[:, 0:8], src))
                    link(dve.match_replace(src, vals[:, 0:8], src, -3.0e38))
                    link(dve.max(vals[:, 8:16], src))
                    link(dve.max_index(idx[:, 8:16], vals[:, 8:16], src))
                for i in range(TT):
                    for n in range(2 * H):
                        top16(sc[:, i, n], v[:, i, n], ix[:, i, n])
                link(dve.tensor_copy(ixf[:], ix[:]))
                for i in range(TT):
                    for h in range(H):
                        c = cand[:, h % 2]
                        link(dve.tensor_tensor(c, col_bc(v[:, i, 2 * h], TOPK), row_bc(v[:, i, 2 * h + 1], TOPK), ALU.add))
                        top16(c.rearrange("p a b -> p (a b)"), top[:, i, h], pos[:, i, h])
                flat = top[:].rearrange("p i h r -> p (i h) r")
                link(dve.tensor_copy(stat[:], top[:, :, :, 0]))
                dve.tensor_tensor(flat, flat, col_bc(stat[:].rearrange("p i h -> p (i h)"), TOPK), ALU.subtract).then_inc(apart, 1)
                dve.wait_ge(exped, 1)
                link(dve.tensor_reduce(stat[:].rearrange("p i h -> p (i h)"), flat, AX.X, ALU.add))
                link(dve.reciprocal(stat[:], stat[:]))
                link(dve.tensor_tensor(flat, flat, col_bc(stat[:].rearrange("p i h -> p (i h)"), TOPK), ALU.mult))
                link(dve.tensor_scalar(pa[:], pos[:], 4, None, ALU.logical_shift_right))
                link(dve.tensor_copy(pf[:, 0], pa[:]))
                link(dve.tensor_scalar(pa[:], pos[:], 15, None, ALU.bitwise_and))
                link(dve.tensor_copy(pf[:, 1], pa[:]))
                for m in range(2):
                    for i in range(TT):
                        f = hot[:].rearrange("p h r a -> p (h r) a")
                        dve.wait_ge(chosen, 2 * m + i)
                        link(dve.tensor_tensor(f, col_bc(pf[:, m, i].rearrange("p h r -> p (h r)"), TOPK), row_bc(k.iota[:, 0:TOPK], H * TOPK), ALU.is_equal))
                        keys = ixf[:, i].rearrange("p (h c) r -> p h c r", c=2)[:, :, m, :].unsqueeze(2).to_broadcast([P, H, TOPK, TOPK])
                        link(dve.tensor_tensor(hot[:], hot[:], keys, ALU.mult))
                        dve.tensor_reduce(key[:, m, i].rearrange("p h r -> p (h r)"), f, AX.X, ALU.add).then_inc(chosen, 1)

            @block.scalar
            def _(act):
                act.wait_ge(apart, 1)
                act.activation(top[:], top[:], ACT.Exp).then_inc(exped, 1)
                act.wait_ge(turned, 1)
                for n, out in enumerate((i1t, i2t, gt)):
                    act.activation(out[:], half(k.ps, n), ACT.Copy).then_inc(moved, 1)

            @block.tensor
            def _(pe):
                pe.wait_ge(chosen, 4)
                for n, src in enumerate((key[:, 0], key[:, 1], top[:])):
                    for i in range(TT):
                        mm = pe.transpose(half(k.ps, n)[:, i * P:(i + 1) * P], src[:, i].rearrange("p h r -> p (h r)"), k.ident)
                mm.then_inc(turned, 1)


def peer_grid(k, grid, i1t, i2t, gt):
    Q = 8
    with ExitStack() as ctx:
        free = k.ring[:, (k.start["peer"] + 2) % R, :].rearrange("p (q j) -> p q j", j=NK)
        first, second = free[:, 0:Q], free[:, Q:2 * Q]
        with k.stage("peer_grid") as st:
            block = st.block
            made_a, made_b, multiplied, moved = st.signals(4)

            @block.gpsimd
            def _(pool):
                st.clear_last(pool)

            @block.vector
            def _(dve):
                with dve.Fori(0, T // Q) as it:
                    for q in range(Q):
                        if q % 4 == 0:
                            dve.wait_ge(multiplied, it * 2 + (q // 4 + 1))
                        t = bass.ds(it * Q + q, 1)
                        dve.tensor_scalar(first[:, q], k.iota, i1t[:, t], gt[:, t], ALU.is_equal, ALU.mult).then_inc(made_a, 1)
                        dve.tensor_scalar(second[:, q], k.iota, i2t[:, t], None, ALU.is_equal).then_inc(made_b, 1)

            @block.tensor
            def _(pe):
                pe.sem_inc(multiplied, 2)
                with pe.Fori(0, T // Q) as it:
                    for b in range(2):
                        pe.wait_ge(made_a, it * Q + 4 * b + 4)
                        pe.wait_ge(made_b, it * Q + 4 * b + 4)
                        pe.wait_ge(moved, it * 2 + (b + 1))
                        for q in range(4):
                            mm = pe.matmul(k.ps[:, b, q * P:(q + 1) * P], first[:, 4 * b + q], second[:, 4 * b + q], start=True, stop=True)
                        mm.then_inc(multiplied, 1)

            @block.scalar
            def _(act):
                act.sem_inc(moved, 2)
                with act.Fori(0, T // Q) as it:
                    for b in range(2):
                        act.wait_ge(multiplied, it * 2 + b + 3)
                        act.activation(grid[:, :, bass.ds(it * Q + 4 * b, 4)], k.ps[:, b, :].rearrange("p (q j) -> p j q", q=4), ACT.Copy).then_inc(moved, 1)


def peer_experts(k, grid, dt):
    g0 = k.start["peer"]
    with ExitStack() as ctx:
        zrow = k.sb("zero_row", [1, P], ctx=ctx)
        co = k.sb("peer_coef", [P, 2, T], ctx=ctx)
        zero = co[:].rearrange("p a t -> p (a t)")
        with k.stage("peer_experts") as st:
            block = st.block
            zeroed, turned, act_moved, dve_moved, z_ready, gelued, weighed, summed, z_half, chain, out_done = st.signals(11)
            acc = [half(k.ps, 8 + j) for j in range(KC)]
            NP = NK // 2

            @block.gpsimd
            def _(pool):
                st.clear_last(pool)
                pool.memset(zrow[:], 0.0).then_inc(zeroed, 1)
                pool.memset(zero, 0.0).then_inc(zeroed, 1)

            @block.sync
            def _(sp):
                k.issue(sp, g0 + NP + R)

            def over(eng, step):
                for j in range(2 * R):
                    step(j, 0)
                with eng.Fori(1, NP // R) as it:
                    for j in range(2 * R):
                        step(j, it)
                for j in range(2 * (NP % R)):
                    step(j, NP // R)

            def first_step(j, it):
                return isinstance(it, int) and it == 0 and j == 0

            def last_step(j, it):
                return isinstance(it, int) and it == NP // R and j == 2 * (NP % R) - 1

            @block.tensor
            def _(pe):
                pe.wait_ge(zeroed, 2)
                for b in range(4):
                    mm = pe.matmul(k.ps[:, 4 + b, :], zero[:, 0:P], zero, start=True, stop=False, skip_group_check=True)
                mm.then_inc(summed, 1)

                def turn(j, it, n):
                    s = (g0 + j // 2) % R
                    if j % 2 == 0:
                        pe.wait_ge(k.loaded[s], k.load_value(g0 + j // 2, it, 2))
                    pe.wait_ge(act_moved, n)
                    pe.wait_ge(dve_moved, n)
                    for c in range(KC):
                        mm = pe.transpose(k.ps[:, c // 4, (c % 4) * P:(c % 4 + 1) * P],
                                          k.ring[:, s, (j % 2) * D + c * P:(j % 2) * D + (c + 1) * P], k.ident)
                    mm.then_inc(turned, 1)

                def up(j, it, n):
                    s = (g0 + j // 2) % R
                    pe.wait_ge(weighed, n + 1)
                    for c in range(KC):
                        off = 2 * D + (j % 2) * D + c * P
                        mm = pe.matmul(acc[c], k.ring[:, s, off:off + P], co[:, j % 2], start=False, stop=False, skip_group_check=True)
                    mm.then_inc(summed, 1) if j % 2 == 0 else mm.then_inc(k.used, 1)

                turn(0, 0, 0)

                def step(j, it):
                    n = it * (2 * R) + j
                    pe.wait_ge(act_moved, n + 1)
                    pe.wait_ge(dve_moved, n + 1)
                    for c in range(KC):
                        mm = pe.matmul(half(k.ps, 4 + 2 * (j % 2)), dt[:, c], k.h[:, c], start=(c == 0), stop=(c == KC - 1))
                    mm.then_inc(z_ready, 1)
                    if not last_step(j, it):
                        turn((j + 1) % (2 * R), it + (1 if j == 2 * R - 1 else 0), n + 1)
                    if not first_step(j, it):
                        up((j - 1) % (2 * R), it - (1 if j == 0 else 0), n - 1)
                over(pe, step)
                up(2 * (NP % R) - 1, NP // R, NK - 1)
                for b in range(4):
                    mm = pe.matmul(k.ps[:, 4 + b, :], zrow[:], k.ones[0:1, 0:1].to_broadcast([1, 512]), start=False, stop=True,
                                   skip_group_check=True)
                mm.then_inc(out_done, 1)

            @block.scalar
            def _(act):
                def move(n):
                    act.wait_ge(turned, n + 1)
                    act.activation(dt[:, 0:4], k.ps[:, 0, :].rearrange("p (c e) -> p c e", c=4), ACT.Copy).then_inc(act_moved, 1)
                move(0)

                def step(j, it):
                    n = it * (2 * R) + j
                    act.wait_ge(z_ready, n + 1)
                    if not last_step(j, it):
                        move(n + 1)
                    if j % 2 == 0:
                        act.wait_ge(summed, it * R + (j // 2 + 1))
                    else:
                        act.wait_ge(k.used, it * R + (g0 + j // 2))
                    act.activation(co[:, j % 2], half(k.ps, 4 + 2 * (j % 2)), ACT.Gelu).then_inc(gelued, 1)
                over(act, step)

            @block.vector
            def _(dve):
                def move(n):
                    dve.wait_ge(turned, n + 1)
                    dve.tensor_copy(dt[:, 4:8], k.ps[:, 1, :].rearrange("p (c e) -> p c e", c=4)).then_inc(dve_moved, 1)
                move(0)

                def step(j, it):
                    n = it * (2 * R) + j
                    dve.wait_ge(z_ready, n + 1)
                    if not last_step(j, it):
                        move(n + 1)
                    dve.wait_ge(gelued, n + 1)
                    dve.tensor_tensor(co[:, j % 2:j % 2 + 1], co[:, j % 2:j % 2 + 1], grid[:, bass.ds(n, 1)], ALU.mult).then_inc(weighed, 1)
                over(dve, step)
                dve.wait_ge(out_done, 1)
                for c in range(KC):
                    dve.tensor_tensor(k.xT[:, c], k.xT[:, c], acc[c], ALU.add).then_inc(chain, 1)


def store(k, out):
    with ExitStack() as ctx:
        rows = k.sb("out_rows", [P, TT, D], ctx=ctx)
        with k.stage("store") as st:
            block = st.block
            turned, moved, stored = st.signals(3)

            @block.gpsimd
            def _(pool):
                st.clear_last(pool)

            @block.tensor
            def _(pe):
                for i in range(TT):
                    for c in range(KC):
                        mm = pe.transpose(k.ps[:, 2 * i + c // 4, (c % 4) * P:(c % 4 + 1) * P], k.xT[:, c, i * P:(i + 1) * P], k.ident)
                    mm.then_inc(turned, 1)

            @block.scalar
            def _(act):
                for i in range(TT):
                    act.wait_ge(turned, i + 1)
                    act.activation(rows[:, i].rearrange("p (b n) -> p b n", b=2), k.ps[:, 2 * i:2 * i + 2, :], ACT.Copy).then_inc(moved, 1)

            @block.sync
            def _(sp):
                for i in range(TT):
                    sp.wait_ge(moved, i + 1)
                    sp.dma_start(out[0, i * P:(i + 1) * P, :], rows[:, i, :]).then_inc(stored, 16)
                sp.wait_ge(stored, 16 * TT)


def setup(k):
    a = k.a
    k.ring = k.sb("weight_ring", [P, R, SLOT])
    k.xT = k.sb("residual", [P, KC, T])[:]
    k.h = k.sb("hidden_in", [P, KC, T])[:]
    k.cols = k.sb("param_cols", [P, NPT, P])
    k.col_at = {}
    k.mod = k.sb("mod", [P, L, 48])
    k.c_act = k.sb("c_act", [P, KC])
    k.hp = k.sb("head_params", [SSH, 6])
    k.nega = k.sb("minus_a", [SSH, 6])
    k.wba = k.sb("w_beta_a", [P, L, KC, 16])
    k.wdt = k.sb("w_dt", [P, KC, 16])
    k.wrt = k.sb("w_router", [P, KC, NE])
    k.rb = k.sb("b_router", [1, NE])
    at = constants()[1]
    width = sum(w for _, w in at.values())
    k.tables = k.sb("tables", [P, width])

    def table(n):
        return k.tables[:, at[n][0]:at[n][0] + at[n][1]]
    k.ident, k.ones, k.tri_ge, k.ones64 = table("ident"), table("ones"), table("tri_ge"), table("ones64")
    k.neg_le, k.msk_lt, k.neg_lt = table("neg_le"), table("msk_lt"), table("neg_lt")
    k.iota, k.perm, k.inv = table("iota"), table("perm"), table("inv")

    def col(name, i, n):
        tile, r0 = k.col_at[name]
        return k.cols[:, tile, r0 + i:r0 + i + n]
    k.col = col

    def cols512(name, n, w, c0=0):
        v = w.rearrange("(c p) n -> p c n", p=P)

        def loads(q, it, slot):
            yield slot.rearrange("p (c n) -> p c n", c=KC), v[:, :, bass.ds(it * (512 * R) + (c0 + 512 * q), 512)]
        k.add_group(name, n, loads)

    def rows1024(name, n, kb, w):
        v = w.rearrange("(b p) n -> p b n", p=P)

        def loads(q, it, slot):
            yield slot[:, 0:kb * D].rearrange("p (b n) -> p b n", b=kb), v[:, bass.ds(it * (kb * R) + kb * q, kb), :]
        k.add_group(name, n, loads)

    def ffn(name, rounds, w1, w3, w2):
        v1, v3 = w1.rearrange("(c p) n -> p c n", p=P), w3.rearrange("(c p) n -> p c n", p=P)
        v2 = w2.rearrange("(b p) n -> p b n", p=P)

        def loads(q, it, slot):
            if q < 2:
                yield slot.rearrange("p (c n) -> p c n", c=KC), (v1, v3)[q][:, :, bass.ds(it * 512, 512)]
            else:
                yield slot.rearrange("p (b n) -> p b n", b=4), v2[:, bass.ds(it * 4, 4), :]
        k.add_group(name, R * rounds, loads)

    cols512("ada0", 12, a["ada_w"][0])
    cols512("ada1", 12, a["ada_w"][1])
    for l in range(L):
        cols512(f"in_a{l}", 8, a["w_in"][l])
        cols512(f"in_b{l}", 7, a["w_in"][l], IN_B)
        cols512(f"up_dn{l}", 2, a["w_up_dn"][l])
        rows1024(f"up_sb{l}", 1, 4, a["w_up_sb"][l])
        cols512(f"out{l}", 2, a["w_out"][l])
        if l == 0:
            ffn("ffn", 7, a["ffn_w1"][0], a["ffn_w3"][0], a["ffn_w2"][0])
        else:
            ffn("moe", 7 * NE, a["moe_w1"][0][0], a["moe_w3"][0][0], a["moe_w2"][0][0])
    cols512("mem_kv", 3, a["w_mem_kv_2"][0])
    cols512("in2_a", 6, a["w_in_2"][0])
    cols512("in2_b", 12, a["w_in_2"][0], IN2_B)
    cols512("br_ssd", 2, a["w_ssd_br_2"][0])
    rows1024("br_dil", 1, 2, a["w_dil_br_2"][0])
    rows1024("br_mem", 2, 3, a["w_mem_br_2"][0])
    cols512("out2", 2, a["w_out_2"][0])
    cols512("peer_query", 4, a["peer_w_query_2"][0])
    down = a["peer_down_2"][0].rearrange("(i j) d -> i j d", j=NK)
    up = a["peer_up_2"][0].rearrange("(i j) d -> i j d", j=NK)

    def loads(q, it, slot):
        js = bass.ds(it * (2 * R) + 2 * q, 2)
        yield slot[:, 0:2 * D].rearrange("p (j d) -> p j d", j=2), down[:, js, :]
        yield slot[:, 2 * D:4 * D].rearrange("p (j d) -> p j d", j=2), up[:, js, :]
    k.add_group("peer", NK // 2, loads, 2)


def program(nc, a, out):
    with ExitStack() as ctx:
        k = Kern(nc, ctx, a)
        setup(k)
        prologue(k)
        modulation(k)
        for l in range(L):
            with ExitStack() as lc:
                k.o = k.sb(f"branch_out{l}", [P, 16, T], ctx=lc)[:]
                k.proj = k.sb(f"projected{l}", [P, NBLK1, T], ctx=lc)[:]
                rms(k, f"norm_mix{l}", k.xT, k.h, k.mod[:, l, 8:16], k.mod[:, l, 0:8])
                linear(k, f"in_a{l}", 8, k.h, k.proj, 0)
                linear(k, f"in_b{l}", 7, k.h, k.proj, 32)
                delta_rule(k, l)
                stick_breaking(k, l)
                s = k.start
                branches(k, f"branches{l}", [([(s[f"up_dn{l}"], None), (s[f"up_dn{l}"] + 1, None)], 0),
                                             ([(s[f"up_sb{l}"], 4)], 8)], (GD0, GS0), s[f"out{l}"], k.mod[:, l, 16:24])
            rms(k, f"norm_ffn{l}", k.xT, k.h, k.mod[:, l, 32:40], k.mod[:, l, 24:32])
            if l == 0:
                ffn(k, k.mod[:, l, 40:48])
            else:
                with ExitStack() as lc:
                    weight = k.sb("expert_weight", [P, NE, T], ctx=lc)
                    gathered = k.sb("expert_tokens", [P, KC, NE * P], ctx=lc)
                    scatter = k.sb("expert_scatter", [P, NE, T], ctx=lc)
                    largest = k.sb("expert_largest", [1, 1], I32, ctx=lc)
                    router(k, weight, gathered, scatter, largest)
                    moe(k, k.mod[:, l, 40:48], weight, gathered, scatter, largest)
        rms(k, "final_norm", k.xT, k.xT, k.col("final_norm", 0, 8))
        second_mixer(k)
        rms(k, "norm_peer", k.xT, k.h, k.col("norm_ffn_2", 0, 8))
        peer(k)
        store(k, out)


def second_mixer(k):
    with ExitStack() as ctx:
        mk = k.sb("mem_k", [P, 6, T], ctx=ctx)
        mv = k.sb("mem_v", [P, TT, 6 * P], ctx=ctx)
        memory_keys(k, mk, mv)
        k.o = k.sb("branch_out2", [P, 16, T], ctx=ctx)[:]
        k.proj = k.sb("projected2", [P, NBLK2, T], ctx=ctx)[:]
        rms(k, "norm_mix2", k.xT, k.h, k.col("norm_mix_2", 0, 8))
        linear(k, "in2_a", 6, k.h, k.proj, 0)
        linear(k, "in2_b", 12, k.h, k.proj, 24)
        ssd(k)
        dilated(k)
        memory_attention(k, mk, mv)
        s = k.start
        branches(k, "branches2", [([(s["br_ssd"], None), (s["br_ssd"] + 1, None)], 0), ([(s["br_dil"], 2)], 8),
                                  ([(s["br_mem"], 3), (s["br_mem"] + 1, 3)], 10)], (G20, G20 + 8, G20 + 16), s["out2"], None)


def peer(k):
    with ExitStack() as ctx:
        turned = k.sb("down_turned", [P, KC, P], ctx=ctx)
        i1t, i2t, gt = (turned[:, 2 * n:2 * n + 2].rearrange("p a b -> p (a b)") for n in range(3))
        peer_choice(k, i1t, i2t, gt)
        grid = k.sb("pair_grid", [P, NK, T], ctx=ctx)
        peer_grid(k, grid, i1t, i2t, gt)
        peer_experts(k, grid, turned)


_INS = ["x", "c", "ada_w", "ada_b", "norm_mix", "norm_ffn", "w_in", "conv_w", "dn_a_log", "dn_dt_bias", "dn_out_norm",
        "w_up_dn", "w_up_sb", "w_out", "ffn_w1", "ffn_w3", "ffn_w2", "router_w", "router_b", "moe_w1", "moe_w3", "moe_w2",
        "final_norm", "mem_2", "positions_2", "norm_mix_w_2", "w_in_2", "ssd_conv_w_2", "ssd_conv_b_2", "ssd_dt_bias_2",
        "ssd_a_log_2", "ssd_d_2", "ssd_norm_w_2", "dil_q_norm_w_2", "dil_k_norm_w_2", "mem_norm_w_2", "w_mem_kv_2",
        "mem_q_norm_w_2", "mem_k_norm_w_2", "w_ssd_br_2", "w_dil_br_2", "w_mem_br_2", "w_out_2", "norm_ffn_w_2",
        "peer_w_query_2", "peer_sub_keys_2", "peer_down_2", "peer_up_2"]


def kernel(**inputs):
    import concourse.bacc as bacc
    from concourse.bass_utils import run_bass_kernel_spmd

    nc = bacc.Bacc("TRN2", target_bir_lowering=False, num_devices=1)
    main, _, level, memh, dil = constants()
    given = {n: np.ascontiguousarray(inputs[n]) for n in _INS}
    given.update(table_main=main, table_level=level, table_memh=memh, table_dil=dil)
    arrays, args = {}, {}
    for name, v in given.items():
        arrays[f"in_{name}"] = v
        args[name] = nc.dram_tensor(f"in_{name}", v.shape, mybir.dt.from_np(v.dtype), kind="ExternalInput").ap()
    out = nc.dram_tensor("out_tokens", (1, T, D), F32, kind="ExternalOutput").ap()
    program(nc, args, out)
    r = run_bass_kernel_spmd(nc, [arrays], core_ids=[0])
    return np.asarray(r.results[0]["out_tokens"])
```
